# Optimizing a Trainium2 kernel written in Bass

```python
import math
import jax, jax.numpy as jnp
from jax import lax
import numpy as np

D_MODEL = 2048
BATCH = 1
SEQ = 512
DEPTH = 1

CHUNK = 64
N_PREV_CHUNKS = 8
BAND = (N_PREV_CHUNKS + 1) * CHUNK
ATTN_HEADS = 8
ATTN_HEAD_DIM = 128
ATTN_WIDTH = ATTN_HEADS * ATTN_HEAD_DIM
REL_CLIP = 128
SSM_WIDTH = D_MODEL // 2
SSM_GROUP = 16
SSM_GROUPS = SSM_WIDTH // SSM_GROUP
SSM_STATE = 64
DT_MIN = 0.001
DT_MAX = 0.1
IN_SPLITS = (ATTN_WIDTH, 2 * ATTN_WIDTH, 3 * ATTN_WIDTH, 3 * ATTN_WIDTH + SSM_WIDTH,
             3 * ATTN_WIDTH + SSM_WIDTH + D_MODEL)
IN_WIDTH = 3 * ATTN_WIDTH + SSM_WIDTH + 2 * D_MODEL
PEER_HEADS = 8
PEER_NKEYS = 128
PEER_EXPERTS = PEER_NKEYS * PEER_NKEYS
PEER_HALF = 128
PEER_QDIM = 2 * PEER_HALF
PEER_TOPK = 16
PEER_BLOCK = 128
PLE_DIM = 256
LN_EPS = 1e-5

kernel_name = "hybrid_chunk_attn_s5_peer_deepnorm"

def layer_norm(x, g, b):
    xf = x.astype(jnp.float32)
    mu = jnp.mean(xf, axis=-1, keepdims=True)
    var = jnp.mean(jnp.square(xf - mu), axis=-1, keepdims=True)
    y = (xf - mu) * lax.rsqrt(var + LN_EPS)
    return (y * g + b).astype(x.dtype)

def rms_norm(x, g):
    xf = x.astype(jnp.float32)
    y = xf * lax.rsqrt(jnp.mean(jnp.square(xf), axis=-1, keepdims=True) + LN_EPS)
    return (y * g).astype(x.dtype)

def chunk_attention(q, k, v, rel_bias):
    b, s, h, dh = q.shape
    nc = s // CHUNK
    pad = N_PREV_CHUNKS * CHUNK
    kp = jnp.pad(k, ((0, 0), (pad, 0), (0, 0), (0, 0)))
    vp = jnp.pad(v, ((0, 0), (pad, 0), (0, 0), (0, 0)))
    q_pos = jnp.arange(CHUNK)
    k_pos = jnp.arange(BAND)
    rel = (pad + q_pos)[:, None] - k_pos[None, :]
    rel_idx = jnp.clip(rel, -REL_CLIP, REL_CLIP) + REL_CLIP
    bias = rel_bias[:, rel_idx].astype(jnp.float32)
    scale = dh ** -0.5
    qc = q.reshape(b, nc, CHUNK, h, dh).transpose(1, 0, 2, 3, 4)

    def one_chunk(args):
        c, qb = args
        start = c * CHUNK
        kb = lax.dynamic_slice_in_dim(kp, start, BAND, axis=1)
        vb = lax.dynamic_slice_in_dim(vp, start, BAND, axis=1)
        sc = jnp.einsum('bqhd,bkhd->bhqk', qb, kb).astype(jnp.float32) * scale + bias
        valid = (start - pad + k_pos) >= 0
        sc = jnp.where(valid, sc, -1e30)
        w = jax.nn.softmax(sc, axis=-1).astype(vb.dtype)
        return jnp.einsum('bhqk,bkhd->bqhd', w, vb)

    out = lax.map(one_chunk, (jnp.arange(nc), qc))
    return out.transpose(1, 0, 2, 3, 4).reshape(b, s, h * dh)

def _complex_affine_combine(e1, e2):
    a1r, a1i, b1r, b1i = e1
    a2r, a2i, b2r, b2i = e2
    ar = a1r * a2r - a1i * a2i
    ai = a1r * a2i + a1i * a2r
    br = a2r * b1r - a2i * b1i + b2r
    bi = a2r * b1i + a2i * b1r + b2i
    return (ar, ai, br, bi)

def s5_scan(u, lam_re, lam_im, log_dt, b_re, b_im, c_re, c_im, d_skip):
    s = u.shape[1]
    lr = lam_re.astype(jnp.float32)
    li = lam_im.astype(jnp.float32)
    dt = jnp.exp(log_dt.astype(jnp.float32))[:, None]
    mag = jnp.exp(lr * dt)
    ab_re = mag * jnp.cos(li * dt)
    ab_im = mag * jnp.sin(li * dt)
    nr = ab_re - 1.0
    ni = ab_im
    den = lr * lr + li * li
    f_re = (nr * lr + ni * li) / den
    f_im = (ni * lr - nr * li) / den
    br = b_re.astype(jnp.float32)
    bi = b_im.astype(jnp.float32)
    bb_re = f_re[..., None] * br - f_im[..., None] * bi
    bb_im = f_re[..., None] * bi + f_im[..., None] * br
    uf = u.astype(jnp.float32)
    bu_re = jnp.einsum('bsgh,gph->bsgp', uf, bb_re)
    bu_im = jnp.einsum('bsgh,gph->bsgp', uf, bb_im)
    g, p_dim = ab_re.shape
    a_re = jnp.broadcast_to(ab_re, (1, s, g, p_dim))
    a_im = jnp.broadcast_to(ab_im, (1, s, g, p_dim))
    _, _, h_re, h_im = lax.associative_scan(
        _complex_affine_combine, (a_re, a_im, bu_re, bu_im), axis=1)
    y = (jnp.einsum('ghp,bsgp->bsgh', c_re.astype(jnp.float32), h_re)
         - jnp.einsum('ghp,bsgp->bsgh', c_im.astype(jnp.float32), h_im)
         + d_skip.astype(jnp.float32) * uf)
    return y.astype(u.dtype)

def mixer(h, w_in, rel_bias, lam_re, lam_im, log_dt, b_re, b_im, c_re, c_im, d_skip,
          w_ssm_glu, w_attn_up, w_ssm_up, w_out):
    b, s, _ = h.shape
    z = h @ w_in
    q, k, v, u, g_attn, g_ssm = jnp.split(z, IN_SPLITS, axis=-1)
    hd = (b, s, ATTN_HEADS, ATTN_HEAD_DIM)
    y_attn = chunk_attention(q.reshape(hd), k.reshape(hd), v.reshape(hd), rel_bias)
    y_ssm = s5_scan(u.reshape(b, s, SSM_GROUPS, SSM_GROUP), lam_re, lam_im, log_dt,
                    b_re, b_im, c_re, c_im, d_skip).reshape(b, s, SSM_WIDTH)
    y_ssm = jax.nn.gelu(y_ssm)
    y_ssm = y_ssm * jax.nn.sigmoid(y_ssm @ w_ssm_glu)
    merged = (jax.nn.sigmoid(g_attn) * (y_attn @ w_attn_up)
              + jax.nn.sigmoid(g_ssm) * (y_ssm @ w_ssm_up))
    return merged @ w_out

def peer_ffn(h, w_q, sub_keys, u_table, v_table):
    b, s, d = h.shape
    q = (h @ w_q).reshape(b, s, PEER_HEADS, 2, PEER_HALF)
    sc = jnp.einsum('bsrch,rckh->bsrck', q, sub_keys).astype(jnp.float32)
    v_half, i_half = lax.top_k(sc, PEER_TOPK)
    cand = v_half[..., 0, :, None] + v_half[..., 1, None, :]
    cand_idx = i_half[..., 0, :, None] * PEER_NKEYS + i_half[..., 1, None, :]
    cand = cand.reshape(b, s, PEER_HEADS, PEER_TOPK * PEER_TOPK)
    cand_idx = cand_idx.reshape(b, s, PEER_HEADS, PEER_TOPK * PEER_TOPK)
    top_sc, pos = lax.top_k(cand, PEER_TOPK)
    experts = jnp.take_along_axis(cand_idx, pos, axis=-1)
    gates = jax.nn.softmax(top_sc, axis=-1)
    nb = s // PEER_BLOCK
    hb = h.reshape(b, nb, PEER_BLOCK, d).transpose(1, 0, 2, 3)
    eb = experts.reshape(b, nb, PEER_BLOCK, PEER_HEADS, PEER_TOPK).transpose(1, 0, 2, 3, 4)
    gb = gates.reshape(b, nb, PEER_BLOCK, PEER_HEADS, PEER_TOPK).transpose(1, 0, 2, 3, 4)

    def apply_block(args):
        hk, ek, gk = args
        u = u_table[ek]
        act = jax.nn.gelu(jnp.einsum('btd,btrkd->btrk', hk, u).astype(jnp.float32))
        w = (gk * act).astype(hk.dtype)
        return jnp.einsum('btrk,btrkd->btd', w, v_table[ek])

    y = lax.map(apply_block, (hb, eb, gb))
    return y.transpose(1, 0, 2, 3).reshape(b, s, d)

def setup_inputs(seed: int = 0) -> dict:
    key = jax.random.key(seed)
    ks = jax.random.split(key, 32)
    f32 = jnp.float32
    beta = (8.0 * DEPTH) ** -0.25
    nrm = lambda k, shape, sc: jax.random.normal(k, shape, f32) * sc
    L = DEPTH
    lam_im0 = jnp.broadcast_to(math.pi * jnp.arange(SSM_STATE, dtype=f32), (L, SSM_GROUPS, SSM_STATE))
    return {
        "x": nrm(ks[0], (BATCH, SEQ, D_MODEL), 1.0),
        "p": nrm(ks[1], (DEPTH, BATCH, SEQ, PLE_DIM), 1.0),
        "ln_in_g": 1.0 + nrm(ks[2], (D_MODEL,), 0.02),
        "ln_in_b": nrm(ks[3], (D_MODEL,), 0.02),
        "w_in": nrm(ks[4], (L, D_MODEL, IN_WIDTH), D_MODEL ** -0.5),
        "attn_rel_bias": nrm(ks[5], (L, ATTN_HEADS, 2 * REL_CLIP + 1), 0.1),
        "ssm_lam_re": -0.5 + nrm(ks[6], (L, SSM_GROUPS, SSM_STATE), 0.01),
        "ssm_lam_im": lam_im0 + nrm(ks[7], (L, SSM_GROUPS, SSM_STATE), 0.01),
        "ssm_log_dt": jax.random.uniform(ks[8], (L, SSM_GROUPS), f32,
                                         math.log(DT_MIN), math.log(DT_MAX)),
        "ssm_b_re": nrm(ks[9], (L, SSM_GROUPS, SSM_STATE, SSM_GROUP), (2 * SSM_GROUP) ** -0.5),
        "ssm_b_im": nrm(ks[10], (L, SSM_GROUPS, SSM_STATE, SSM_GROUP), (2 * SSM_GROUP) ** -0.5),
        "ssm_c_re": nrm(ks[11], (L, SSM_GROUPS, SSM_GROUP, SSM_STATE), SSM_STATE ** -0.5),
        "ssm_c_im": nrm(ks[12], (L, SSM_GROUPS, SSM_GROUP, SSM_STATE), SSM_STATE ** -0.5),
        "ssm_d": nrm(ks[13], (L, SSM_GROUPS, SSM_GROUP), 1.0),
        "w_ssm_glu": nrm(ks[14], (L, SSM_WIDTH, SSM_WIDTH), SSM_WIDTH ** -0.5),
        "w_attn_up": nrm(ks[15], (L, ATTN_WIDTH, D_MODEL), ATTN_WIDTH ** -0.5),
        "w_ssm_up": nrm(ks[16], (L, SSM_WIDTH, D_MODEL), SSM_WIDTH ** -0.5),
        "w_mix_out": nrm(ks[17], (L, D_MODEL, D_MODEL), beta * D_MODEL ** -0.5),
        "ln1_g": 1.0 + nrm(ks[18], (L, D_MODEL), 0.02),
        "ln1_b": nrm(ks[19], (L, D_MODEL), 0.02),
        "w_peer_q": nrm(ks[20], (L, D_MODEL, PEER_HEADS * PEER_QDIM), D_MODEL ** -0.5),
        "peer_sub_keys": nrm(ks[21], (L, PEER_HEADS, 2, PEER_NKEYS, PEER_HALF), PEER_HALF ** -0.5),
        "peer_u": nrm(ks[22], (L, PEER_EXPERTS, D_MODEL), D_MODEL ** -0.5),
        "peer_v": nrm(ks[23], (L, PEER_EXPERTS, D_MODEL), beta * PEER_HEADS ** -0.5),
        "ple_w_in": nrm(ks[24], (L, PLE_DIM, D_MODEL), PLE_DIM ** -0.5),
        "ple_norm_g": 1.0 + nrm(ks[25], (L, D_MODEL), 0.02),
        "ple_w_gate": nrm(ks[26], (L, D_MODEL, D_MODEL), D_MODEL ** -0.5),
        "ln2_g": 1.0 + nrm(ks[27], (L, D_MODEL), 0.02),
        "ln2_b": nrm(ks[28], (L, D_MODEL), 0.02),
    }

def reference(x, p, ln_in_g, ln_in_b, w_in, attn_rel_bias, ssm_lam_re, ssm_lam_im, ssm_log_dt,
              ssm_b_re, ssm_b_im, ssm_c_re, ssm_c_im, ssm_d, w_ssm_glu, w_attn_up, w_ssm_up,
              w_mix_out, ln1_g, ln1_b, w_peer_q, peer_sub_keys, peer_u, peer_v, ple_w_in,
              ple_norm_g, ple_w_gate, ln2_g, ln2_b):
    alpha = (2.0 * DEPTH) ** 0.25
    h = layer_norm(x, ln_in_g, ln_in_b)
    for i in range(DEPTH):
        mix = mixer(h, w_in[i], attn_rel_bias[i], ssm_lam_re[i], ssm_lam_im[i], ssm_log_dt[i],
                    ssm_b_re[i], ssm_b_im[i], ssm_c_re[i], ssm_c_im[i], ssm_d[i],
                    w_ssm_glu[i], w_attn_up[i], w_ssm_up[i], w_mix_out[i])
        h = layer_norm(alpha * h + mix, ln1_g[i], ln1_b[i])
        ple = rms_norm(p[i] @ ple_w_in[i], ple_norm_g[i]) * jax.nn.sigmoid(h @ ple_w_gate[i])
        ffn = peer_ffn(h, w_peer_q[i], peer_sub_keys[i], peer_u[i], peer_v[i])
        h = layer_norm(alpha * h + ffn + ple, ln2_g[i], ln2_b[i])
    return h


_drawn_inputs = setup_inputs


def setup_inputs(seed=0):
    import zlib

    import numpy as np

    out = dict(_drawn_inputs(seed))
    spreads = {}
    factors = {'attn_rel_bias': 36.285,
     'ssm_lam_re': 64.0,
     'ssm_lam_im': 42.064,
     'ssm_log_dt': 41.8,
     'ssm_b_re': 53.272,
     'ssm_b_im': 53.816,
     'ssm_c_re': 53.512,
     'ssm_c_im': 50.704,
     'ple_norm_g': 58.865,
     'ln2_g': 22.447,
     'ln2_b': 21.762,
     'ln_in_g': 5.188,
     'ln_in_b': 5.285,
     'w_ssm_glu': 3.689,
     'w_attn_up': 2.73,
     'ln1_g': 15.664,
     'ln1_b': 15.82}
    for name, (base, spread) in spreads.items():
        noise = np.random.default_rng([zlib.crc32(name.encode()), seed]).standard_normal(out[name].shape)
        drawn = base * np.exp(spread * noise) if base else spread * noise
        out[name] = __import__('jax').numpy.asarray(drawn.astype(out[name].dtype))
    for name, factor in factors.items():
        out[name] = (out[name] * factor).astype(out[name].dtype)
    return out
```

```python
import concourse.bass as bass
import numpy as np
from concourse import mybir

F32 = mybir.dt.float32
F32R = mybir.dt.float32r
U32 = mybir.dt.uint32
ALU = mybir.AluOpType
ACT = mybir.ActivationFunctionType
AX = mybir.AxisListType

P = 128
S = 512
D = 2048
TT = S // P
DC = D // P
HEADS, DH = 8, 128
W2 = 1024
WC = W2 // P
GROUPS, GCH, ST = 64, 16, 64
LC = 8
NC = S // LC
CB_G = 8
CB_Q = CB_G // 2
QN = GROUPS // 2
RH, NK, TOPK = 8, 128, 16
EB = NK
SB = EB // 4
HOT = 8
HOT_FROM = 2
HOT_ITER = S // (4 * HOT)
PLE = 256
EPS = 1e-5
ALPHA = 2.0 ** 0.25
SCALE = DH ** -0.5

SL = 2048
HALF = SL // 2
N_IN = 64
N_GLU = 4
N_UP = 16
N_OUT, N_Q, N_GATE = 16, 16, 16
N_U, N_V = 128, 128
AT_GLU = N_IN
AT_UP = AT_GLU + N_GLU
AT_OUT = AT_UP + N_UP
AT_Q = AT_OUT + N_OUT
AT_GATE = AT_Q + N_Q
AT_U = AT_GATE + N_GATE
AT_V = AT_U + N_U
N_SLABS = AT_V + N_V
BLK_GLU = N_IN + 1
BLK_UP = BLK_GLU + 2 * N_GLU
BLK_OUT = BLK_UP + 2 * N_UP
BLK_Q = BLK_OUT + N_OUT
BLK_GATE = BLK_Q + N_Q
BLK_U = BLK_GATE + N_GATE
BLK_V = BLK_U + N_U

TWO_PI_1 = 6.28125
TWO_PI_2 = float(np.round((2 * np.pi - TWO_PI_1) * 2.0**19) / 2.0**19)
TWO_PI_3 = float(2 * np.pi - TWO_PI_1 - TWO_PI_2)
ROUND = 1.5 * 2.0**23
PI_F32 = 3.1415925


def fact(n):
    return float(np.prod(np.arange(1, n + 1, dtype=np.float64)))


def build_trunk(nc, x, p_t, vecs, weights, band_ext, lam_re, lam_im, log_dt, b_in, c_in, d_skip,
                keys_t, ple_w, out):
    kb = 1024
    base = 1152
    ring_at, a_at = base, base + 48 * kb
    c_at = a_at + 64 * kb
    k_at = c_at + 32 * kb
    w_at = k_at + 2 * kb

    def sb(name, shape, at, dt=F32):
        return nc.alloc_sbuf_tensor_at(name, shape, dt, offset=int(at))

    def w(name, shape, at_kb, dt=F32):
        return sb(name, shape, w_at + at_kb * kb, dt)

    raw = [sb(f"raw{i}", [P, SL], ring_at + 8 * kb * i) for i in range(2)]
    whi = [sb(f"whi{i}", [P, SL], ring_at + 16 * kb + 8 * kb * i, F32R) for i in range(2)]
    wlo = [sb(f"wlo{i}", [P, SL], ring_at + 32 * kb + 8 * kb * i, F32R) for i in range(2)]
    h0_hi = sb("h0_hi", [P, DC, S], a_at, F32R)
    h0_lo = sb("h0_lo", [P, DC, S], a_at + 32 * kb, F32R)
    xt = sb("xt", [P, TT, D], c_at)
    y_attn = sb("y_attn", [P, WC, S], c_at)
    y_ssm = sb("y_ssm", [P, WC, S], c_at + 16 * kb)
    ident = sb("ident", [P, P], k_at)
    iota = sb("iota", [P, P], k_at + 512)
    stat = sb("stat", [P, TT, 4, 6], k_at + 1024)
    mv = sb("mv", [P, TT, 2], k_at + 1408)
    std = sb("std", [P, TT], k_at + 1440)
    rstd = sb("rstd", [P, TT], k_at + 1472)
    shift = sb("shift", [P, TT], k_at + 1504)
    row_max = sb("row_max", [P, TT], k_at + 1536)
    neg_max = sb("neg_max", [P, TT], k_at + 1568)
    row_sum = sb("row_sum", [P, TT], k_at + 1600)
    row_rec = sb("row_rec", [P, TT], k_at + 1632)
    g_in = w("g_in", [P, D], 0)
    b_ln_in = w("b_ln_in", [P, D], 8)
    q_h = w("q_h", [P, S], 0)
    k_h = w("k_h", [P, S], 2)
    v_h = w("v_h", [P, S], 4)
    v_keys = w("v_keys", [P, TT, DH], 6)
    prob = w("prob", [P, TT, S], 8)
    u_sc = w("u_sc", [P, CB_G, NC], 16)
    g_out = [w(f"g_out{i}", [P, S], 18 + 2 * i) for i in range(2)]
    toep = w("toep", [P, CB_G, P], 22)
    y_sc = w("y_sc", [P, CB_G, NC], 26)
    y_cs = w("y_cs", [P, LC, NC], 28)
    t1 = w("t1", [P, 640], 30)
    t2 = w("t2", [P, 640], 32.5)
    in_map = w("in_map", [P, 2, CB_Q, P], 35)
    prob_t = w("prob_t", [P, TT, S], 39)
    e_tab = w("e_tab", [P, 2, CB_Q, LC, GCH], 39)
    u_cs = w("u_cs", [P, LC, NC], 43)
    f_tab = w("f_tab", [P, 2, CB_Q, LC + 1, GCH], 47)
    h_st = w("h_st", [P, 2, CB_Q, NC + 1], 51.5)
    k_tab = w("k_tab", [GCH, CB_G, P], 54)
    pow_up = w("pow_up", [P, 2, QN, LC + 1], 58)
    pow_dn = w("pow_dn", [P, 2, QN, LC + 1], 60.5)
    lev = w("lev", [P, 2, QN, 6], 63)
    bb = w("bb", [P, 2, QN, GCH], 64.5)
    c_s = w("c_s", [P, 2, CB_Q, GCH], 68.5)
    bb_s = w("bb_s", [P, 2, CB_Q, GCH], 69)
    pow_up_s = w("pow_up_s", [P, 2, CB_Q, LC + 1], 69.5)
    pow_dn_s = w("pow_dn_s", [P, 2, CB_Q, LC + 1], 70)
    lev_s = w("lev_s", [P, 2, CB_Q, 6], 70.5)
    band = w("band", [P, 2 * P], 71)
    d_bc = w("d_bc", [GCH, W2], 72)
    d_diag = w("d_diag", [GCH, CB_G, GCH], 76)
    prm = w("prm", [P, 20, QN], 39)
    b_raw = w("b_raw", [P, 2, QN, GCH], 41.5)

    ya_hi = sb("ya_hi", [P, WC, S], a_at, F32R)
    ya_lo = sb("ya_lo", [P, WC, S], a_at + 16 * kb, F32R)
    y2_hi = sb("y2_hi", [P, WC, S], a_at + 32 * kb, F32R)
    y2_lo = sb("y2_lo", [P, WC, S], a_at + 48 * kb, F32R)
    res = sb("res", [P, TT, D], a_at)
    emb = sb("emb", [P, TT, D], a_at + 32 * kb)
    gate_st = [sb(f"gate_st{i}", [P, SB, 16, 4], a_at + (32 + 8 * i) * kb) for i in range(2)]
    act_out = [sb(f"act_out{i}", [P, S], a_at + (48 + 2 * i) * kb) for i in range(2)]
    hot_j = sb("hot_j", [P, HOT, P], a_at + 52 * kb, F32R)
    hot_g = sb("hot_g", [P, HOT, 2, P], a_at + 56 * kb, F32R)
    ys_hi = w("ys_hi", [P, WC, S], 0, F32R)
    ys_lo = w("ys_lo", [P, WC, S], 16, F32R)
    glu_s = [w(f"glu_s{i}", [P, S], 32 + 2 * i) for i in range(2)]
    glu_y = w("glu_y", [P, S], 36)
    m_hi = w("m_hi", [P, DC, S], 0, F32R)
    m_lo = w("m_lo", [P, DC, S], 32, F32R)
    h1_hi = w("h1_hi", [P, DC, S], 0, F32R)
    h1_lo = w("h1_lo", [P, DC, S], 32, F32R)
    up_a = w("up_a", [P, S], 64)
    up_s = w("up_s", [P, S], 66)
    up_m = w("up_m", [P, S], 68)
    p_sb = w("p_sb", [P, 2, S], 64)
    junk = w("junk", [P, S], 68)
    emb_add = w("emb_add", [P, TT, P], 64)
    mt = [w(f"mt{i}", [P, S], 70 + 2 * i) for i in range(2)]
    top_v = w("top_v", [P, TT, TOPK], 74)
    top_i = w("top_i", [P, TT, TOPK], 74.25, U32)
    pos_a = w("pos_a", [P, TT, TOPK], 74.5, U32)
    pos_b = w("pos_b", [P, TT, TOPK], 74.75, U32)
    pos_af = w("pos_af", [P, TT, TOPK], 75)
    pos_bf = w("pos_bf", [P, TT, TOPK], 75.25)
    sq_sum = w("sq_sum", [P, TT, 4], 75.5)
    sq_tot = w("sq_tot", [P, TT], 75.625)
    sq_rec = w("sq_rec", [P, TT], 75.75)
    gate_sum = w("gate_sum", [P, TT * RH], 75.875)
    gate_rec = w("gate_rec", [P, TT * RH], 76)
    gates = [sb(f"gates{i}", [P, 2, S], c_at + 4 * kb * i) for i in range(2)]
    ln_g = sb("ln_g", [P, D], c_at)
    ln_b = sb("ln_b", [P, D], c_at + 8 * kb)
    pw_sb = sb("pw_sb", [P, 2, D], c_at + 16 * kb)
    emb_g = sb("emb_g", [P, D], c_at)
    keys = sb("keys", [P, 2 * RH, NK], c_at + 8 * kb)
    v_all = sb("v_all", [P, TT, 2 * RH, TOPK], c_at + 16 * kb)
    i_all = sb("i_all", [P, TT, 2 * RH, TOPK], c_at + 20 * kb)
    rest = sb("rest", [P, TT, NK], c_at + 24 * kb)
    sel_i = sb("sel_i", [P, TT, P], c_at + 26 * kb)
    sel_j = sb("sel_j", [P, TT, P], c_at + 28 * kb)
    sel_g = sb("sel_g", [P, TT, P], c_at + 30 * kb)
    cand = sb("cand", [P, TT, TOPK, TOPK], c_at)
    cand_rest = sb("cand_rest", [P, TT, TOPK * TOPK], c_at + 4 * kb)
    eq_a = sb("eq_a", [P, TT, TOPK, TOPK], c_at + 8 * kb)
    eq_b = sb("eq_b", [P, TT, TOPK, TOPK], c_at + 12 * kb)
    pick_i = sb("pick_i", [P, S], c_at)
    pick_j = sb("pick_j", [P, S], c_at + 2 * kb)
    pick_gh = sb("pick_gh", [P, S], c_at + 4 * kb, F32R)
    pick_gl = sb("pick_gl", [P, S], c_at + 6 * kb)
    cols = sb("cols", [P, 4, 4 * HOT], c_at + 8 * kb)
    act_in = [sb("act_in0", [P, 4, S], c_at), w("act_in1", [P, 4, S], 0)]
    gate_in = [sb("gate_in0", [P, S, 4], c_at + 8 * kb), w("gate_in1", [P, S, 4], 8)]
    ew_hi = [sb("ew_hi0", [P, 4, S], c_at + 16 * kb, F32R), w("ew_hi1", [P, 4, S], 16, F32R)]
    ew_lo = [sb("ew_lo0", [P, 4, S], c_at + 24 * kb, F32R), w("ew_lo1", [P, 4, S], 24, F32R)]
    ew = sb("ew", [P, 4, S], a_at + 56 * kb)
    ln2_g = w("ln2_g", [P, D], 32)
    ln2_b = w("ln2_b", [P, D], 40)

    ps = [nc.alloc_psum_tensor(f"bank{i}", [P, S], F32) for i in range(8)]
    ps_p, ps_s, ps_t, ps_x, ps_y = ps[0:2], ps[2:4], ps[4:6], ps[6], ps[7]

    def hot_in(m):
        return ps[2 + m][:, :].rearrange("p (t z b i) -> p z b t i", t=2, z=2, i=4)

    def hot_out(s, m):
        at = HOT * (s % 2) + 2 * m
        return gate_st[s // 2][:, :, at:at + 2, :]

    def dram(name, shape):
        return nc.dram_tensor(name, shape, F32, kind="Internal").ap()

    h0_d = dram("h0_d", [TT, P, D])
    gate_d = dram("gate_d", [2 * DC, P, S])
    u_d = dram("u_d", [P, LC, NC])
    k_d = dram("k_d", [GCH, CB_G, (2 * LC - 1) * GCH])
    act_d = dram("act_d", [SB, P, 4, S])
    pick_d = dram("pick_d", [SB, P, S * 4])
    band_d = dram("band_d", [HEADS, P, 2 * P])
    y_d = dram("y_d", [P, CB_G, NC])

    sem = {}

    def sm(name):
        sem[name] = nc.alloc_semaphore(name)
        return sem[name]

    raw_landed = [sm("raw_landed0"), sm("raw_landed1")]
    hi_made, lo_made, blk_done, evac = sm("hi_made"), sm("lo_made"), sm("blk_done"), sm("evac")
    x_landed = [sm(f"x_landed{i}") for i in range(TT)]
    ln_in_landed, ident_made = sm("ln_in_landed"), sm("ident_made")
    var_ready, std_ready, rstd_ready = sm("var_ready"), sm("std_ready"), sm("rstd_ready")
    xn_ready, h_ready, turned = sm("xn_ready"), sm("h_ready"), sm("turned")
    turn_hi, turn_lo, h0_stored = sm("turn_hi"), sm("turn_lo"), sm("h0_stored")
    prm_landed, dt_ready, prm_ready = sm("prm_landed"), sm("dt_ready"), sm("prm_ready")
    c_landed, ef_made, band_landed = sm("c_landed"), sm("ef_made"), sm("band_landed")
    u_stored, u_landed = sm("u_stored"), sm("u_landed")
    e_turned, in_map_made, k_done, k_made = sm("e_turned"), sm("in_map_made"), sm("k_done"), sm("k_made")
    k_zeroed, k_stored, toep_landed = sm("k_zeroed"), sm("k_stored"), sm("toep_landed")
    bu_done, h_filled, scanned, y_done = sm("bu_done"), sm("h_filled"), sm("scanned"), sm("y_done")
    y_made, y_stored, y_landed = sm("y_made"), sm("y_stored"), sm("y_landed")
    qkv_made, v_turned, v_made = sm("qkv_made"), sm("v_turned"), sm("v_made")
    sc_done, max_made, exp_made, prob_made = sm("sc_done"), sm("max_made"), sm("exp_made"), sm("prob_made")
    pt_done, pt_made, pv_done = sm("pt_done"), sm("pt_made"), sm("pv_done")
    g_stored = [sm("g_stored0"), sm("g_stored1")]
    band_laid = sm("band_laid")
    split_hi_made, split_lo_made, glu_made = sm("split_hi_made"), sm("split_lo_made"), sm("glu_made")
    gates_landed = [sm("gates_landed0"), sm("gates_landed1")]
    sig_made, merged, res_landed = sm("sig_made"), sm("merged"), sm("res_landed")
    mt_turned, mt_used = sm("mt_turned"), sm("mt_used")
    ple_landed, ln1_landed, pw_done, pw_evac = sm("ple_landed"), sm("ln1_landed"), sm("pw_done"), sm("pw_evac")
    keys_landed, emb_g_landed = sm("keys_landed"), sm("emb_g_landed")
    ms_ready, rms_ready = sm("ms_ready"), sm("rms_ready")
    picks_made, exps_made, gates_made, picks_turned = sm("picks_made"), sm("exps_made"), sm("gates_made"), sm("picks_turned")
    pick_gh_made = sm("pick_gh_made")
    hot_made, hot_done, hot_moved, hot_evac = sm("hot_made"), sm("hot_done"), sm("hot_moved"), sm("hot_evac")
    pick_stored = [sm("pick_stored0"), sm("pick_stored1")]
    act_stored = [sm("act_stored0"), sm("act_stored1")]
    aux_landed = [sm("aux_landed0"), sm("aux_landed1")]
    ew_made, v_done, v_added = sm("ew_made"), sm("v_done"), sm("v_added")
    ln2_landed, out_stored = sm("ln2_landed"), sm("out_stored")
    branch_made = sm("branch_made")

    block = nc.Block()
    with block:

        @block.sync
        def _(sp):
            def load_slab(n, slot):
                sp.wait_ge(lo_made, 2 * n + 1)
                sp.dma_start(raw[slot][:, :], weights[bass.ds(n, 1), :, :].rearrange("a p n -> (a p) n")
                             ).then_inc(raw_landed[slot], 16)

            for t in range(TT):
                sp.dma_start(xt[:, t, :], x[t * P:(t + 1) * P, :]).then_inc(x_landed[t], 16)
            sp.dma_start(g_in[:, :], vecs[0:1, :].rearrange('a d -> (a d)').partition_broadcast(P)).then_inc(ln_in_landed, 16)
            sp.dma_start(b_ln_in[:, :], vecs[1:2, :].rearrange('a d -> (a d)').partition_broadcast(P)).then_inc(ln_in_landed, 16)
            sp.dma_start(prm[:, 0, :], lam_re).then_inc(prm_landed, 16)
            sp.dma_start(prm[:, 1, :], lam_im).then_inc(prm_landed, 16)
            for r in range(2):
                sp.dma_start(prm[ST * r:ST * (r + 1), 2, :], log_dt[r].partition_broadcast(ST)
                             ).then_inc(prm_landed, 16)
            sp.dma_start(b_raw[:, :, :, :], b_in).then_inc(prm_landed, 16)
            sp.dma_start(d_bc[:, :], d_skip.partition_broadcast(GCH)).then_inc(prm_landed, 16)

            sp.dma_start(band_d, bass.AP(band_ext.tensor, 127, [[384, HEADS], [-1, P], [1, 2 * P]])
                         ).then_inc(band_laid, 16)
            sp.wait_ge(band_laid, 16)

            with sp.Fori(0, HEADS) as i:
                sp.wait_ge(ef_made, i + 1)
                sp.dma_start(c_s[:, :, :, :], c_in[bass.ds(i, 1)].rearrange("a p r q c -> (a p) r q c")
                             ).then_inc(c_landed, 16)
                for b in range(8):
                    load_slab(8 * i + b, b % 2)
                    if b == 3:
                        sp.wait_ge(max_made, TT * i + 1)
                        bias = band_d[bass.ds(i, 1)].rearrange("a p n -> (a p) n")
                        sp.dma_start(band[:, 0:192], bias[:, 0:192]).then_inc(band_landed, 16)
                        sp.dma_start(band[64:P, 192:256], bias[64:P, 192:256]).then_inc(band_landed, 16)

            def row(j):
                return vecs[j:j + 1, :].rearrange("a d -> (a d)").partition_broadcast(P)

            with sp.Fori(AT_GLU // 2, AT_UP // 2) as j:
                for s in range(2):
                    load_slab(2 * j + s, s)
            with sp.Fori(AT_UP // 2, AT_OUT // 2) as j:
                for s in range(2):
                    load_slab(2 * j + s, s)
            with sp.Fori(AT_OUT // 2, AT_Q // 2 - 2) as j:
                for s in range(2):
                    load_slab(2 * j + s, s)
            sp.wait_ge(merged, DC + 1)
            sp.dma_start(ln_g[:, :], row(2)).then_inc(ln1_landed, 16)
            sp.dma_start(ln_b[:, :], row(3)).then_inc(ln1_landed, 16)
            sp.dma_start(pw_sb[:, :, :], ple_w).then_inc(ple_landed, 16)
            sp.dma_start(p_sb[:, :, :], p_t).then_inc(ple_landed, 16)
            with sp.Fori(AT_Q // 2 - 2, AT_Q // 2 + 1) as j:
                for s in range(2):
                    load_slab(2 * j + s, s)
            sp.wait_ge(h_ready, 2 * TT)
            sp.wait_ge(pw_evac, 16)
            sp.dma_start(emb_g[:, :], row(4)).then_inc(emb_g_landed, 16)
            sp.dma_start(keys[:, :, :], keys_t).then_inc(keys_landed, 16)
            slabs_then = (AT_U + 4 * (HOT_FROM + HOT_ITER + 3)) // 2
            with sp.Fori(AT_Q // 2 + 1, slabs_then) as j:
                for s in range(2):
                    load_slab(2 * j + s, s)

            def load_aux(sbn, k):
                sp.dma_start(act_in[k][:, :, :], act_d[bass.ds(sbn, 1)].rearrange("a p b t -> (a p) b t")
                             ).then_inc(aux_landed[k], 16)
                sp.dma_start(gate_in[k][:, :, :].rearrange("p t i -> p (t i)"),
                             pick_d[bass.ds(sbn, 1)].rearrange("a p n -> (a p) n")).then_inc(aux_landed[k], 16)

            for h in range(2):
                sp.wait_ge(pick_stored[h], 16 * (HOT_ITER + 1))
                sp.wait_ge(act_stored[h], 16 * 3)
            load_aux(0, 0)
            with sp.Fori(slabs_then, AT_V // 2 + 1) as j:
                for s in range(2):
                    load_slab(2 * j + s, s)

            def expert_pair(j, last):
                for k in range(2):
                    n = AT_V + 8 * j + 4 * k
                    load_slab(n + 2, 0)
                    load_slab(n + 3, 1)
                    if not (last and k == 1):
                        sp.wait_ge(blk_done, BLK_V)
                        for h in range(2):
                            sp.wait_ge(act_stored[h], 16 * (EB // 2 + 1))
                        sp.wait_ge(ew_made, 2 * j + k + 1)
                        load_aux(2 * j + k + 1, (k + 1) % 2)
                        load_slab(n + 4, 0)
                        load_slab(n + 5, 1)

            with sp.Fori(0, SB // 2 - 1) as j:
                expert_pair(j, False)
            sp.dma_start(ln2_g[:, :], row(5)).then_inc(ln2_landed, 16)
            sp.dma_start(ln2_b[:, :], row(6)).then_inc(ln2_landed, 16)
            expert_pair(SB // 2 - 1, True)
            for t in range(TT):
                sp.wait_ge(h_ready, 2 * TT + t + 1)
                sp.dma_start(out[t * P:(t + 1) * P, :], res[:, t, :]).then_inc(out_stored, 16)
            sp.wait_ge(out_stored, 16 * TT)
            sp.wait_ge(h0_stored, 16 * TT)

        @block.gpsimd
        def _(pool):
            pool.memset(ident[:, :], 0.0)
            pool.iota(iota[:, :], [[1, P]], base=0, channel_multiplier=0,
                      allow_small_or_imprecise_dtypes=True)
            pool.drain()
            pool.affine_select(out=ident[:, :], in_=ident[:, :], compare_op=ALU.not_equal, fill=1.0, base=0,
                               pattern=[[-1, P]], channel_multiplier=1).then_inc(ident_made, 1)
            pool.sem_inc(lo_made, 3)
            for counter, credits in ((evac, 2), (mt_turned, 2), (mt_used, 2), 
                                     (v_added, 8), (blk_done, 1), (ef_made, 1), (max_made, 1), (pv_done, 1),
                                     (glu_made, 1), (merged, 1), (ew_made, 1), (v_done, 1), (g_stored[0], 16),
                                     (g_stored[1], 16), (k_stored, 16), (act_stored[0], 16), (act_stored[1], 16),
                                     (pick_stored[0], 16),
                                     (pick_stored[1], 16)):
                pool.sem_inc(counter, credits)
            with pool.Fori(0, N_SLABS // 2) as j:
                for slot in range(2):
                    for half in range(2):
                        part = slice(half * HALF, (half + 1) * HALF)
                        pool.wait_ge(hi_made, 4 * j + 2 * slot + half + 1)
                        pool.tensor_tensor(wlo[slot][:, part], raw[slot][:, part],
                                           whi[slot][:, part].bitcast(F32), ALU.subtract).then_inc(lo_made, 1)

        @block.scalar
        def _(act):
            copy = ACT.Copy

            def normalise(tiles, first):
                act.wait_ge(var_ready, first)
                act.activation(std[:, :], std[:, :], ACT.Sqrt).then_inc(std_ready, 1)
                act.wait_ge(rstd_ready, first)
                for t in range(TT):
                    act.activation(tiles[:, t, :], tiles[:, t, :], ACT.Identity, bias=shift[:, t:t + 1],
                                   scale=rstd[:, t:t + 1]).then_inc(xn_ready, 1)

            def turned_hi(dst, first):
                for t in range(TT):
                    for g in range(4):
                        act.wait_ge(turned, 16 * first + 4 * t + g + 1)
                        act.activation(dst[:, 4 * g:4 * g + 4, t * P:(t + 1) * P],
                                       ps[4 * (t % 2) + g][:, :].rearrange("p (c t) -> p c t", c=4),
                                       copy).then_inc(turn_hi, 1)

            act.wait_ge(prm_landed, 16 * 6)
            act.activation(prm[:, 2, :], prm[:, 2, :], ACT.Exp).then_inc(dt_ready, 1)
            normalise(xt, 1)
            for t in range(TT):
                act.wait_ge(h_ready, t + 1)
                act.dma_start(h0_d[t], xt[:, t, :]).then_inc(h0_stored, 16)
            turned_hi(h0_hi, 0)
            act.wait_ge(k_zeroed, 1)
            act.dma_start(k_d[:, :, 0:(LC - 1) * GCH], k_tab[:, :, 0:(LC - 1) * GCH]).then_inc(k_zeroed, 16)
            act.wait_ge(k_zeroed, 17)

            act.wait_ge(prm_ready, 1)
            act.wait_ge(raw_landed[0], 16)
            for half in range(2):
                part = slice(half * HALF, (half + 1) * HALF)
                act.activation(whi[0][:, part], raw[0][:, part], copy).then_inc(hi_made, 1)
            with act.Fori(0, HEADS) as i:
                def step(b):
                    nxt = b + 1
                    slot = nxt % 2
                    act.wait_ge(raw_landed[slot], 16 * (4 * i + nxt // 2 + 1))
                    act.wait_ge(blk_done, 8 * i + b + 1)
                    for half in range(2):
                        cols = slice(half * HALF, (half + 1) * HALF)
                        act.activation(whi[slot][:, cols], raw[slot][:, cols], copy).then_inc(hi_made, 1)
                    act.wait_ge(blk_done, 8 * i + b + 2)

                def store_gate(j):
                    act.wait_ge(g_stored[j % 2], 16 * (2 * i + j // 2 + 1))
                    act.activation(g_out[j % 2][:, :], ps_p[j % 2][:, :], copy)
                    act.drain()
                    act.dma_start(gate_d[bass.ds(4 * i + j, 1)].rearrange("a p n -> (a p) n"),
                                  g_out[j % 2][:, :]).then_inc(g_stored[j % 2], 16)

                step(0)
                act.activation(u_cs[:, :, :], ps_p[0][:, :].rearrange("p (c s) -> p s c", s=LC), copy)
                act.drain()
                act.dma_start(u_d, u_cs[:, :, :]).then_inc(u_stored, 16)

                step(1)
                act.activation(q_h[:, :], ps_p[1][:, :], copy).then_inc(qkv_made, 1)
                act.wait_ge(e_turned, i + 1)
                for ri in range(2):
                    last = act.activation(in_map[:, ri, :, :], ps_t[ri][:, :].rearrange("p (q n) -> p q n", q=CB_Q),
                                          copy)
                last.then_inc(in_map_made, 1)
                act.wait_ge(u_stored, 16 * (i + 1))
                for s in range(LC):
                    act.dma_start(u_sc[GCH * s:GCH * (s + 1), :, :],
                                  u_d.rearrange("(g c) s n -> s c g n", c=GCH)[s]).then_inc(u_landed, 16)

                step(2)
                act.activation(k_h[:, :], ps_p[0][:, :], copy).then_inc(qkv_made, 1)
                act.wait_ge(k_made, i + 1)
                act.dma_start(k_d[:, :, (LC - 1) * GCH:], k_tab[:, :, :]).then_inc(k_stored, 16)
                act.wait_ge(bu_done, i + 1)
                act.activation(h_st[:, :, :, 1:], ps_s[0][:, :].rearrange("p (r q n) -> p r q n", r=2, q=CB_Q),
                               copy).then_inc(h_filled, 1)

                step(3)
                act.activation(v_h[:, :], ps_p[1][:, :], copy).then_inc(qkv_made, 1)
                act.wait_ge(k_stored, 16 * (i + 2))
                for s in range(LC):
                    act.dma_start(toep[GCH * s:GCH * (s + 1), :, :],
                                  k_d[:, :, (LC - 1 - s) * GCH:(LC - 1 - s) * GCH + P]).then_inc(toep_landed, 16)

                step(4)
                store_gate(0)

                step(5)
                store_gate(1)
                act.wait_ge(v_turned, i + 1)
                act.activation(v_keys[:, :, :], ps_t[0][:, :].rearrange("p (k n) -> p k n", k=TT),
                               copy).then_inc(v_made, 1)

                def exps(t):
                    n = (t + 1) * P
                    act.wait_ge(max_made, TT * i + t + 2)
                    act.activation(prob[:, t, 0:n], prob[:, t, 0:n], ACT.Exp, bias=neg_max[:, t:t + 1],
                                   accum_out=row_sum[:, t:t + 1]).then_inc(exp_made, 1)

                exps(0)
                exps(1)

                step(6)
                store_gate(2)
                act.wait_ge(y_done, i + 1)
                for r, bank in ((0, ps_x), (1, ps_y)):
                    act.activation(y_sc[:, r::2, :], bank[:, 0:CB_Q * NC].rearrange("p (q n) -> p q n", q=CB_Q),
                                   copy)
                act.drain()
                act.dma_start(y_d, y_sc[:, :, :]).then_inc(y_stored, 16)
                exps(2)
                exps(3)
                for t in range(TT):
                    act.wait_ge(pt_done, TT * i + t + 1)
                    act.activation(prob_t[:, 0:t + 1, t * P:(t + 1) * P],
                                   ps_t[t % 2][:, 0:(t + 1) * P].rearrange("p (k n) -> p k n", n=P),
                                   copy).then_inc(pt_made, 1)

                step(7)
                store_gate(3)
                act.wait_ge(y_stored, 16 * (i + 1))
                for g in range(CB_G):
                    act.dma_start(y_cs[GCH * g:GCH * (g + 1), :, :],
                                  y_d.rearrange("(s c) g n -> g c s n", c=GCH)[g]).then_inc(y_landed, 16)
                act.wait_ge(pv_done, i + 2)
                act.activation(y_attn[:, bass.ds(i, 1), :], ps_y[:, :].unsqueeze(1), copy)
                act.wait_ge(y_landed, 128 * (i + 1))
                act.activation(y_ssm[:, bass.ds(i, 1), :].rearrange("p o (c s) -> p (o s) c", s=LC),
                               y_cs[:, :, :], ACT.Gelu_apprx_tanh).then_inc(branch_made, 1)
            act.wait_ge(g_stored[0], 16 * (2 * HEADS + 1))
            act.wait_ge(g_stored[1], 16 * (2 * HEADS + 1))
            act.wait_ge(branch_made, HEADS)
            act.activation(ys_hi[:, :, :], y_ssm[:, :, :], copy).then_inc(split_hi_made, 1)
            act.activation(ya_hi[:, :, :], y_attn[:, :, :], copy).then_inc(split_hi_made, 1)

            def next_hi(at, j, s, used_sem, used):
                slot = (s + 1) % 2
                act.wait_ge(raw_landed[slot], 16 * (at // 2 + j + 1 + s))
                act.wait_ge(used_sem, used)
                for half in range(2):
                    part = slice(half * HALF, (half + 1) * HALF)
                    act.activation(whi[slot][:, part], raw[slot][:, part], copy).then_inc(hi_made, 1)

            with act.Fori(0, N_GLU // 2) as j:
                for s in range(2):
                    m = 4 * j + 2 * s
                    next_hi(AT_GLU, j, s, blk_done, BLK_GLU + m)
                    act.wait_ge(glu_made, m + 1)
                    for half in range(2):
                        act.wait_ge(blk_done, BLK_GLU + m + half + 1)
                        act.activation(glu_s[half][:, :], ps_p[half][:, :], ACT.Sigmoid).then_inc(evac, 1)

            def load_gates(d, k):
                for h in range(2):
                    act.dma_start(gates[k][:, h, :], gate_d[bass.ds(d + DC * h, 1)].rearrange("a p n -> (a p) n")
                                  ).then_inc(gates_landed[k], 16)

            act.wait_ge(split_lo_made, 2)
            load_gates(0, 0)

            def up_pair(j, last):
                for s in range(2):
                    d = 2 * j + s
                    next_hi(AT_UP, j, s, blk_done, BLK_UP + 2 * d)
                    act.wait_ge(merged, d + 1)
                    if not (last and s == 1):
                        load_gates(d + 1, (s + 1) % 2)
                    act.wait_ge(gates_landed[s], 32 * (j + 1))
                    act.activation(gates[s][:, :, :], gates[s][:, :, :], ACT.Sigmoid).then_inc(sig_made, 1)

            with act.Fori(0, DC // 2 - 1) as j:
                up_pair(j, False)
            up_pair(DC // 2 - 1, True)

            act.wait_ge(blk_done, BLK_OUT)
            act.wait_ge(h0_stored, 16 * TT)
            for t in range(TT):
                act.dma_start(res[:, t, :], h0_d[t]).then_inc(res_landed, 16)

            def projections(at, blk0, o0, func):
                with act.Fori(0, DC // 2) as j:
                    for s in range(2):
                        o = 2 * j + s
                        next_hi(at, j, s, blk_done, blk0 + o)
                        act.wait_ge(blk_done, blk0 + o + 1)
                        act.wait_ge(mt_turned, o0 + o + 1)
                        act.activation(mt[s][:, :], ps_p[s][:, :], func).then_inc(evac, 1)

            projections(AT_OUT, BLK_OUT, 0, copy)

            def embedding_out(q):
                t, c = q // 4, q % 4
                act.wait_ge(pw_done, q + 1)
                bank = ps[2 + q % 2]
                act.activation(emb[:, t, c * 512:(c + 1) * 512], bank[:, :], copy)
                act.drain()
                act.activation(junk[:, :], bank[:, :], ACT.Square,
                               accum_out=sq_sum[:, t, c:c + 1]).then_inc(pw_evac, 1)

            for q in range(8):
                embedding_out(q)
            normalise(res, 2)
            for q in range(8, 16):
                embedding_out(q)
            turned_hi(h1_hi, 1)
            act.wait_ge(ms_ready, 1)
            act.activation(sq_tot[:, :], sq_tot[:, :], ACT.Sqrt).then_inc(rms_ready, 1)
            projections(AT_Q, BLK_Q, N_OUT, copy)
            projections(AT_GATE, BLK_GATE, N_OUT + N_Q, ACT.Sigmoid)

            def experts(j, hots):
                for s in range(4):
                    e = 4 * j + s
                    slot = (s + 1) % 2
                    act.wait_ge(raw_landed[slot], 16 * (AT_U // 2 + 2 * j + (s + 1) // 2 + 1))
                    act.wait_ge(blk_done, BLK_U + e)
                    for half in range(2):
                        part = slice(half * HALF, (half + 1) * HALF)
                        act.activation(whi[slot][:, part], raw[slot][:, part], copy).then_inc(hi_made, 1)
                    act.wait_ge(blk_done, BLK_U + e + 1)
                    if not hots:
                        act.wait_ge(mt_used, N_OUT + N_Q + N_GATE + 2)
                    act.wait_ge(act_stored[s % 2], 16 * (2 * j + s // 2 + 1))
                    act.activation(act_out[s % 2][:, :], ps_p[s % 2][:, :], ACT.Gelu_apprx_tanh).then_inc(evac, 1)
                    act.drain()
                    act.dma_start(act_d[bass.ds(j, 1), :, s, :].rearrange("a p t -> (a p) t"),
                                  act_out[s % 2][:, :]).then_inc(act_stored[s % 2], 16)
                    if hots:
                        it, h = j - HOT_FROM, s // 2
                        if s % 2 == 0:
                            act.wait_ge(pick_stored[h], 16 * (it + 1))
                        act.wait_ge(hot_done, 4 * it + s + 1)
                        for m in range(HOT // 2):
                            last = act.activation(hot_out(s, m), hot_in(m)[:, 0], copy)
                        last.then_inc(hot_moved, 1)
                    if hots and s % 2 == 1:
                        act.wait_ge(hot_evac, 2 * it + h + 1)
                        act.dma_start(pick_d[:, :, bass.ds(64 * (2 * it + h), 64)].rearrange("b p n -> p b n"),
                                      gate_st[h][:, :, :, :].rearrange("p b t i -> p b (t i)")
                                      ).then_inc(pick_stored[h], 16)

            with act.Fori(0, HOT_FROM) as j:
                experts(j, False)
            act.wait_ge(picks_made, 1)
            act.activation(sel_g[:, :, :], sel_g[:, :, :], ACT.Exp).then_inc(exps_made, 1)
            act.wait_ge(picks_turned, 1)
            act.activation(pick_i[:, :], ps_s[0][:, :], copy)
            act.activation(pick_j[:, :], ps_s[1][:, :], copy)
            act.activation(pick_gh[:, :], ps_t[0][:, :], copy).then_inc(pick_gh_made, 1)
            with act.Fori(HOT_FROM, HOT_FROM + HOT_ITER) as j:
                experts(j, True)
            with act.Fori(HOT_FROM + HOT_ITER, SB) as j:
                experts(j, False)

            def expert_pair(j, last):
                for q in range(8):
                    if last and q == 7:
                        continue
                    slot = (q + 1) % 2
                    act.wait_ge(raw_landed[slot], 16 * (AT_V // 2 + 4 * j + (q + 1) // 2 + 1))
                    act.wait_ge(v_done, 4 * (8 * j + q) + 1)
                    for half in range(2):
                        part = slice(half * HALF, (half + 1) * HALF)
                        act.activation(whi[slot][:, part], raw[slot][:, part], copy).then_inc(hi_made, 1)

            with act.Fori(0, SB // 2 - 1) as j:
                expert_pair(j, False)
            expert_pair(SB // 2 - 1, True)
            normalise(res, 3)

        @block.tensor
        def _(pe):
            def block_of(bank, slot, n, rhs_hi, rhs_lo):
                for half in range(2):
                    pe.wait_ge(lo_made, 2 * n + half + 4)
                    for c in range(8 * half, 8 * half + 8):
                        cols = slice(c * P, (c + 1) * P)
                        pe.matmul(bank[:, :], whi[slot][:, cols], rhs_hi[:, c, :], start=c == 0, stop=False)
                        pe.matmul(bank[:, :], whi[slot][:, cols], rhs_lo[:, c, :], start=False, stop=False)
                        last = pe.matmul(bank[:, :], wlo[slot][:, cols], rhs_hi[:, c, :], start=False,
                                         stop=c == DC - 1)
                last.then_inc(blk_done, 1)

            def turn(tiles, first):
                if not first:
                    pe.wait_ge(ident_made, 1)
                for t in range(TT):
                    pe.wait_ge(h_ready, TT * first + t + 1)
                    for g in range(4):
                        if t >= 2:
                            pe.wait_ge(turn_lo, 16 * first + 4 * (t - 2) + g + 1)
                        for c in range(4):
                            last = pe.transpose(ps[4 * (t % 2) + g][:, c * P:(c + 1) * P],
                                                tiles[:, t, (4 * g + c) * P:(4 * g + c + 1) * P], ident[:, :])
                        last.then_inc(turned, 1)

            turn(xt, 0)
            pe.wait_ge(turn_lo, 16)
            with pe.Fori(0, HEADS) as i:
                def blk(b):
                    block_of(ps_p[b % 2], b % 2, 8 * i + b, h0_hi, h0_lo)

                def scores(t):
                    if t >= 2:
                        pe.wait_ge(max_made, TT * i + t)
                    pe.matmul(ps_s[t % 2][:, 0:(t + 1) * P], q_h[:, t * P:(t + 1) * P], k_h[:, 0:(t + 1) * P],
                              start=True, stop=True).then_inc(sc_done, 1)

                blk(0)
                blk(1)
                pe.wait_ge(ef_made, i + 2)
                for ri in range(2):
                    for q in range(CB_Q):
                        last = pe.transpose(ps_t[ri][:, q * P:(q + 1) * P],
                                            e_tab[:, ri, q, :, :].rearrange("p s c -> p (s c)"), ident[:, :])
                last.then_inc(e_turned, 1)
                for r, bank in ((0, ps_x), (1, ps_y)):
                    for q in range(CB_Q):
                        for ri in range(2):
                            last = pe.matmul(bank[0:GCH, q * P:(q + 1) * P],
                                             bb_s[ST * r:ST * (r + 1), ri, q, :],
                                             f_tab[ST * r:ST * (r + 1), ri, q, 0:LC, :].rearrange("p s c -> p (s c)"),
                                             start=ri == 0, stop=ri == 1)
                last.then_inc(k_done, 1)
                blk(2)
                pe.wait_ge(in_map_made, i + 1)
                pe.wait_ge(u_landed, 128 * (i + 1))
                for r in range(2):
                    for ri in range(2):
                        for q in range(CB_Q):
                            col = (ri * CB_Q + q) * NC
                            last = pe.matmul(ps_s[0][ST * r:ST * (r + 1), col:col + NC],
                                             in_map[:, ri, q, ST * r:ST * (r + 1)], u_sc[:, 2 * q + r, :],
                                             start=True, stop=True)
                last.then_inc(bu_done, 1)
                blk(3)
                pe.wait_ge(qkv_made, 3 * i + 2)
                pe.wait_ge(h_filled, i + 1)
                scores(0)
                scores(1)
                blk(4)
                pe.wait_ge(qkv_made, 3 * i + 3)
                for t in range(TT):
                    last = pe.transpose(ps_t[0][:, t * P:(t + 1) * P], v_h[:, t * P:(t + 1) * P], ident[:, :])
                last.then_inc(v_turned, 1)
                blk(5)
                scores(2)
                scores(3)
                pe.wait_ge(toep_landed, 128 * (i + 1))
                pe.wait_ge(scanned, i + 1)
                for r, bank in ((0, ps_x), (1, ps_y)):
                    for q in range(CB_Q):
                        dst = bank[:, q * NC:(q + 1) * NC]
                        pe.matmul(dst, toep[:, 2 * q + r, :], u_sc[:, 2 * q + r, :], start=True, stop=False)
                        for ri in range(2):
                            last = pe.matmul(dst, f_tab[ST * r:ST * (r + 1), ri, q, 1:, :].rearrange("p s c -> p (s c)"),
                                             h_st[ST * r:ST * (r + 1), ri, q, 0:NC], start=False, stop=ri == 1)
                last.then_inc(y_done, 1)
                blk(6)
                pe.wait_ge(v_made, i + 1)
                for t in range(TT):
                    pe.wait_ge(prob_made, TT * i + t + 1)
                    if t >= 2:
                        pe.wait_ge(pt_made, TT * i + t - 1)
                    for k in range(t + 1):
                        last = pe.transpose(ps_t[t % 2][:, k * P:(k + 1) * P], prob[:, t, k * P:(k + 1) * P],
                                            ident[:, :])
                    last.then_inc(pt_done, 1)
                blk(7)
                pe.wait_ge(pt_made, TT * (i + 1))
                for k in range(TT):
                    last = pe.matmul(ps_y[:, k * P:], v_keys[:, k, :], prob_t[:, k, k * P:], start=k == 0,
                                     stop=k == TT - 1)
                last.then_inc(pv_done, 1)

            def two_blocks(n, slot, blk, rhs):
                for half in range(2):
                    pe.wait_ge(lo_made, 2 * n + half + 4)
                    pe.wait_ge(evac, blk - BLK_GLU + half + 1)
                    hi, lo = rhs[half]
                    for c in range(WC):
                        part = slice(half * HALF + c * P, half * HALF + (c + 1) * P)
                        pe.matmul(ps_p[half][:, :], whi[slot][:, part], hi[:, c, :], start=c == 0, stop=False)
                        pe.matmul(ps_p[half][:, :], whi[slot][:, part], lo[:, c, :], start=False, stop=False)
                        last = pe.matmul(ps_p[half][:, :], wlo[slot][:, part], hi[:, c, :], start=False,
                                         stop=c == WC - 1)
                    last.then_inc(blk_done, 1)

            pe.wait_ge(split_lo_made, 1)
            with pe.Fori(0, N_GLU // 2) as j:
                for s in range(2):
                    two_blocks(AT_GLU + 2 * j + s, s, BLK_GLU + 4 * j + 2 * s, [(ys_hi, ys_lo)] * 2)
            pe.wait_ge(split_lo_made, 2)
            pe.wait_ge(glu_made, WC + 1)
            with pe.Fori(0, DC // 2) as j:
                for s in range(2):
                    two_blocks(AT_UP + 2 * j + s, s, BLK_UP + 4 * j + 2 * s, [(ya_hi, ya_lo), (y2_hi, y2_lo)])
            pe.wait_ge(merged, DC + 1)

            def projections(at, blk0, o0, rhs_hi, rhs_lo, second):
                def first(o, s):
                    pe.wait_ge(evac, blk0 + o - BLK_GLU + 1)
                    block_of(ps_p[s], s, at + o, rhs_hi, rhs_lo)

                def then(o, s):
                    pe.wait_ge(evac, blk0 + o - BLK_GLU + 3)
                    pe.wait_ge(mt_used, o0 + o + 1)
                    second(o, s).then_inc(mt_turned, 1)

                first(0, 0)
                with pe.Fori(0, DC // 2 - 1) as j:
                    first(2 * j + 1, 1)
                    then(2 * j, 0)
                    first(2 * j + 2, 0)
                    then(2 * j + 1, 1)
                first(DC - 1, 1)
                then(DC - 2, 0)
                then(DC - 1, 1)

            def turn_block(o, s):
                for t in range(TT):
                    last = pe.transpose(ps_t[s][:, t * P:(t + 1) * P], mt[s][:, t * P:(t + 1) * P], ident[:, :])
                return last

            def key_scores(o, s):
                for t in range(TT):
                    last = pe.matmul(ps_t[s][:, t * P:(t + 1) * P], mt[s][:, t * P:(t + 1) * P],
                                     keys[:, bass.ds(o, 1), :].rearrange("p a n -> p (a n)"), start=True, stop=True)
                return last

            projections(AT_OUT, BLK_OUT, 0, m_hi, m_lo, turn_block)
            pe.wait_ge(ple_landed, 32)
            for q in range(16):
                t, c = q // 4, q % 4
                if q >= 2:
                    pe.wait_ge(pw_evac, q - 1)
                for k in range(2):
                    last = pe.matmul(ps[2 + q % 2][:, :], p_sb[:, k, t * P:(t + 1) * P],
                                     pw_sb[:, k, c * 512:(c + 1) * 512], start=k == 0, stop=k == 1)
                last.then_inc(pw_done, 1)
            pe.wait_ge(pw_evac, 16)
            turn(res, 1)
            pe.wait_ge(turn_lo, 32)
            pe.wait_ge(keys_landed, 16)
            projections(AT_Q, BLK_Q, N_OUT, h1_hi, h1_lo, key_scores)
            projections(AT_GATE, BLK_GATE, N_OUT + N_Q, h1_hi, h1_lo, turn_block)
            def experts(j, hots):
                for s in range(4):
                    e = 4 * j + s
                    pe.wait_ge(evac, BLK_U + e - BLK_GLU + 1)
                    block_of(ps_p[s % 2], s % 2, AT_U + e, h1_hi, h1_lo)
                    if hots:
                        pe.wait_ge(hot_made, e - 4 * HOT_FROM + 1)
                        for k in range(HOT):
                            last = pe.matmul(ps[2 + k // 2][:, (k % 2) * 2 * P:(k % 2 + 1) * 2 * P],
                                             hot_j[:, k, :], hot_g[:, k, :, :].rearrange("p z i -> p (z i)"),
                                             start=True, stop=True)
                        last.then_inc(hot_done, 1)

            with pe.Fori(0, HOT_FROM) as j:
                experts(j, False)
            pe.wait_ge(gates_made, 1)
            for bank, sel in ((ps_s[0], sel_i), (ps_s[1], sel_j), (ps_t[0], sel_g)):
                for t in range(TT):
                    last = pe.transpose(bank[:, t * P:(t + 1) * P], sel[:, t, :], ident[:, :])
            last.then_inc(picks_turned, 1)
            with pe.Fori(HOT_FROM, HOT_FROM + HOT_ITER) as j:
                experts(j, True)
            with pe.Fori(HOT_FROM + HOT_ITER, SB) as j:
                experts(j, False)

            with pe.Fori(0, SB // 2) as j:
                for k in range(2):
                    pe.wait_ge(ew_made, 2 * j + k + 2)
                    for c in range(4):
                        q = 4 * k + c
                        n = AT_V + 8 * j + q
                        slot = q % 2
                        if c == 1:
                            pe.wait_ge(evac, BLK_V - BLK_GLU + 2)
                        for t in range(TT):
                            bank = ps[4 * ((c + 1) % 2) + t]
                            pe.wait_ge(v_added, 4 * (8 * j + q) + t + 1)
                            for b in range(4):
                                if t == 0 and b % 2 == 0:
                                    pe.wait_ge(lo_made, 2 * n + b // 2 + 4)
                                rows = slice(t * P, (t + 1) * P)
                                part = slice(b * 512, (b + 1) * 512)
                                pe.matmul(bank[:, :], ew_hi[k][:, b, rows], whi[slot][:, part], start=b == 0,
                                          stop=False)
                                pe.matmul(bank[:, :], ew_hi[k][:, b, rows], wlo[slot][:, part], start=False,
                                          stop=False)
                                last = pe.matmul(bank[:, :], ew_lo[k][:, b, rows], whi[slot][:, part],
                                                 start=False, stop=b == 3)
                            last.then_inc(v_done, 1)

        @block.vector
        def _(dve):
            def tt(o, a, b, op):
                return dve.tensor_tensor(o, a, b, op)

            def statistics(tiles, first, landed):
                for t in range(TT):
                    if landed is not None:
                        dve.wait_ge(landed[t], 16)
                    for q in range(4):
                        dve.bn_stats(stat[:, t, q, :], tiles[:, t, q * 512:(q + 1) * 512])
                    dve.drain()
                    dve.bn_aggr(mv[:, t, :], stat[:, t, :, :].rearrange("p a b -> p (a b)"))
                dve.drain()
                dve.tensor_scalar(std[:, :], mv[:, :, 1], EPS, None, ALU.add).then_inc(var_ready, 1)
                dve.wait_ge(std_ready, first)
                dve.reciprocal(rstd[:, :], std[:, :])
                dve.drain()
                dve.scalar_tensor_tensor(shift[:, :], mv[:, :, 0], -1.0, rstd[:, :], ALU.mult,
                                         ALU.mult).then_inc(rstd_ready, 1)

            def gain_bias(tiles, g, b, first):
                for t in range(TT):
                    dve.wait_ge(xn_ready, TT * first + t + 1)
                    tt(tiles[:, t, :], tiles[:, t, :], g[:, :], ALU.mult)
                    dve.drain()
                    tt(tiles[:, t, :], tiles[:, t, :], b[:, :], ALU.add).then_inc(h_ready, 1)

            def turned_lo(dst_lo, dst_hi, first):
                for t in range(TT):
                    for g in range(4):
                        dve.wait_ge(turn_hi, 16 * first + 4 * t + g + 1)
                        tt(dst_lo[:, 4 * g:4 * g + 4, t * P:(t + 1) * P],
                           ps[4 * (t % 2) + g][:, :].rearrange("p (c t) -> p c t", c=4),
                           dst_hi[:, 4 * g:4 * g + 4, t * P:(t + 1) * P].bitcast(F32),
                           ALU.subtract).then_inc(turn_lo, 1)

            def cmul(o_re, o_im, a, b, ta, tb, minus_im=False):
                tt(ta, a[0], b[0], ALU.mult)
                tt(tb, a[1], b[1], ALU.mult)
                dve.drain()
                tt(o_re, ta, tb, ALU.subtract)
                dve.drain()
                tt(ta, a[0], b[1], ALU.mult)
                tt(tb, a[1], b[0], ALU.mult)
                dve.drain()
                if minus_im:
                    last = dve.scalar_tensor_tensor(o_im, ta, -1.0, tb, ALU.mult, ALU.subtract)
                else:
                    last = tt(o_im, ta, tb, ALU.add)
                dve.drain()
                return last

            def series(acc, y, y2, coeffs, last):
                dve.tensor_scalar(acc, y2, coeffs[0], None, ALU.mult)
                for c in coeffs[1:-1]:
                    dve.drain()
                    dve.scalar_tensor_tensor(acc, acc, c, y2, ALU.add, ALU.mult)
                dve.drain()
                dve.scalar_tensor_tensor(acc, acc, coeffs[-1], last, ALU.add, ALU.mult)
                dve.drain()

            statistics(xt, 1, x_landed)
            dve.wait_ge(ln_in_landed, 32)
            gain_bias(xt, g_in, b_ln_in, 0)
            turned_lo(h0_lo, h0_hi, 0)

            names = "lr li dt em x k th y y2 sn c1 ar ai nr den fr fi u v w".split()
            reg = {n: prm[:, j, :] for j, n in enumerate(names)}
            R = lambda n: reg[n]
            dve.memset(k_tab[:, :, :], 0.0).then_inc(k_zeroed, 1)
            dve.memset(h_st[:, :, :, 0:1], 0.0)
            dve.memset(band[0:64, 192:256], -1e30)
            dve.wait_ge(dt_ready, 1)
            tt(R("x"), R("lr"), R("dt"), ALU.mult)
            tt(R("th"), R("li"), R("dt"), ALU.mult)
            dve.drain()
            dve.tensor_scalar(R("u"), R("x"), -88.0, 88.0, ALU.max, ALU.min)
            dve.drain()
            dve.tensor_scalar(R("y"), R("u"), 1.0 / 64, None, ALU.mult)
            dve.drain()
            series(R("em"), R("y"), R("y"), [1 / fact(n) for n in range(12, 0, -1)], R("y"))
            for _ in range(6):
                dve.scalar_tensor_tensor(R("em"), R("em"), 2.0, R("em"), ALU.add, ALU.mult)
                dve.drain()
            dve.tensor_scalar(R("k"), R("th"), 1 / (2 * np.pi), ROUND, ALU.mult, ALU.add)
            dve.drain()
            dve.tensor_scalar(R("k"), R("k"), -ROUND, None, ALU.add)
            dve.drain()
            for part in (TWO_PI_1, TWO_PI_2, TWO_PI_3):
                dve.scalar_tensor_tensor(R("th"), R("k"), -part, R("th"), ALU.mult, ALU.add)
                dve.drain()
            dve.tensor_scalar(R("th"), R("th"), -PI_F32, PI_F32, ALU.max, ALU.min)
            dve.drain()
            dve.tensor_scalar(R("y"), R("th"), 0.25, None, ALU.mult)
            dve.drain()
            tt(R("y2"), R("y"), R("y"), ALU.mult)
            dve.drain()
            series(R("sn"), R("y"), R("y2"), [1 / fact(9), -1 / fact(7), 1 / fact(5), -1 / fact(3), 1.0], R("y"))
            series(R("c1"), R("y"), R("y2"), [-1 / fact(10), 1 / fact(8), -1 / fact(6), 1 / fact(4), -0.5],
                   R("y2"))
            for _ in range(2):
                dve.scalar_tensor_tensor(R("u"), R("c1"), 1.0, R("sn"), ALU.add, ALU.mult)
                dve.drain()
                dve.scalar_tensor_tensor(R("c1"), R("sn"), -2.0, R("sn"), ALU.mult, ALU.mult)
                dve.drain()
                dve.tensor_scalar(R("sn"), R("u"), 2.0, None, ALU.mult)
                dve.drain()
            dve.tensor_scalar(R("u"), R("em"), 1.0, None, ALU.add)
            dve.drain()
            dve.scalar_tensor_tensor(R("ar"), R("c1"), 1.0, R("u"), ALU.add, ALU.mult)
            tt(R("ai"), R("sn"), R("u"), ALU.mult)
            tt(R("v"), R("em"), R("c1"), ALU.mult)
            tt(R("nr"), R("em"), R("c1"), ALU.add)
            dve.drain()
            tt(R("nr"), R("nr"), R("v"), ALU.add)
            tt(R("u"), R("lr"), R("lr"), ALU.mult)
            tt(R("w"), R("li"), R("li"), ALU.mult)
            dve.drain()
            tt(R("den"), R("u"), R("w"), ALU.add)
            dve.drain()
            dve.reciprocal(R("den"), R("den"))
            tt(R("u"), R("nr"), R("lr"), ALU.mult)
            tt(R("v"), R("ai"), R("li"), ALU.mult)
            dve.drain()
            tt(R("fr"), R("u"), R("v"), ALU.add)
            dve.drain()
            tt(R("u"), R("ai"), R("lr"), ALU.mult)
            tt(R("v"), R("nr"), R("li"), ALU.mult)
            dve.drain()
            tt(R("fi"), R("u"), R("v"), ALU.subtract)
            tt(R("fr"), R("fr"), R("den"), ALU.mult)
            dve.drain()
            tt(R("fi"), R("fi"), R("den"), ALU.mult)
            dve.drain()
            f_wide = [R(n).unsqueeze(2).to_broadcast([P, QN, GCH]) for n in ("fr", "fi")]
            half_t1 = t1[:, 0:QN * GCH].rearrange("p (q c) -> p q c", c=GCH)
            half_t2 = t2[:, 0:QN * GCH].rearrange("p (q c) -> p q c", c=GCH)
            cmul(bb[:, 0], bb[:, 1], f_wide, [b_raw[:, 0], b_raw[:, 1]], half_t1, half_t2)
            dve.memset(pow_up[:, 0, :, 0:1], 1.0)
            dve.memset(pow_up[:, 1, :, 0:1], 0.0)
            dve.tensor_copy(pow_up[:, 0, :, 1], R("ar"))
            dve.tensor_copy(pow_up[:, 1, :, 1], R("ai"))
            dve.drain()
            for lo, n in ((1, 1), (2, 2), (4, 4)):
                by = [pow_up[:, ri, :, lo:lo + 1].to_broadcast([P, QN, n]) for ri in range(2)]
                ta, tb = (z[:, 0:QN * n].rearrange("p (q n) -> p q n", n=n) for z in (t1, t2))
                cmul(pow_up[:, 0, :, lo + 1:lo + n + 1], pow_up[:, 1, :, lo + 1:lo + n + 1],
                     [pow_up[:, ri, :, 1:n + 1] for ri in range(2)], by, ta, tb)
            for m in range(LC + 1):
                dve.tensor_copy(pow_dn[:, :, :, LC - m:LC - m + 1], pow_up[:, :, :, m:m + 1])
            dve.tensor_copy(lev[:, :, :, 0:1], pow_up[:, :, :, LC:LC + 1]).then_inc(prm_ready, 1)
            dve.drain()
            for k in range(5):
                a = [lev[:, ri, :, k] for ri in range(2)]
                cmul(lev[:, 0, :, k + 1], lev[:, 1, :, k + 1], a, a, t1[:, 0:QN], t2[:, 0:QN])

            with dve.Fori(0, HEADS) as i:
                dve.wait_ge(pv_done, i + 1)
                sl = bass.ds(CB_Q * i, CB_Q)
                dve.tensor_copy(pow_up_s[:, :, :, :], pow_up[:, :, sl, :])
                dve.tensor_copy(pow_dn_s[:, :, :, :], pow_dn[:, :, sl, :])
                dve.tensor_copy(lev_s[:, :, :, :], lev[:, :, sl, :])
                dve.tensor_copy(bb_s[:, :, :, :], bb[:, :, sl, :])
                tt(d_diag[:, :, :],
                   d_bc[:, bass.ds(i * P, P)].rearrange("p (g c) -> p g c", g=CB_G),
                   ident[0:GCH, 0:GCH].unsqueeze(1).to_broadcast([GCH, CB_G, GCH]), ALU.mult)
                dve.drain()
                ta, tb = (z[:, 0:512].rearrange("p (q s c) -> p q s c", q=CB_Q, s=LC) for z in (t1, t2))
                wide = [P, CB_Q, LC, GCH]
                cmul(e_tab[:, 0], e_tab[:, 1],
                     [pow_dn_s[:, ri, :, 1:].unsqueeze(3).to_broadcast(wide) for ri in range(2)],
                     [bb_s[:, ri].unsqueeze(2).to_broadcast(wide) for ri in range(2)], ta, tb)
                dve.wait_ge(c_landed, 16 * (i + 1))
                ta, tb = (z[:, 0:576].rearrange("p (q s c) -> p q s c", q=CB_Q, s=LC + 1) for z in (t1, t2))
                wide = [P, CB_Q, LC + 1, GCH]
                cmul(f_tab[:, 0], f_tab[:, 1],
                     [pow_up_s[:, ri].unsqueeze(3).to_broadcast(wide) for ri in range(2)],
                     [c_s[:, ri].unsqueeze(2).to_broadcast(wide) for ri in range(2)], ta, tb,
                     minus_im=True).then_inc(ef_made, 1)
                dve.wait_ge(k_done, i + 1)
                dve.wait_ge(k_stored, 16 * (i + 1))
                dve.wait_ge(k_zeroed, 17)
                for r, bank in ((0, ps_x), (1, ps_y)):
                    dve.tensor_copy(k_tab[:, r::2, :],
                                    bank[0:GCH, :].rearrange("p (q n) -> p q n", q=CB_Q))
                dve.drain()
                tt(k_tab[:, :, 0:GCH], k_tab[:, :, 0:GCH], d_diag[:, :, :], ALU.add).then_inc(k_made, 1)
                dve.wait_ge(h_filled, i + 1)
                for k in range(6):
                    n = NC - 2**k
                    src = h_st[:, :, :, 1:1 + n]
                    ta, tb = (z[:, 0:512].rearrange("p (r q n) -> p r q n", r=2, q=CB_Q)[:, :, :, 0:n]
                              for z in (t1, t2))
                    a_re, a_im = (lev_s[:, ri, :, k:k + 1].unsqueeze(1).to_broadcast([P, 2, CB_Q, n])
                                  for ri in range(2))
                    tt(ta, src, a_re, ALU.mult)
                    tt(tb, src, a_im, ALU.mult)
                    dve.drain()
                    tt(ta[:, 0], ta[:, 0], tb[:, 1], ALU.subtract)
                    tt(ta[:, 1], ta[:, 1], tb[:, 0], ALU.add)
                    dve.drain()
                    last = tt(h_st[:, :, :, 1 + 2**k:], h_st[:, :, :, 1 + 2**k:], ta, ALU.add)
                    if k == 5:
                        last.then_inc(scanned, 1)
                    dve.drain()
                dve.wait_ge(band_landed, 32 * (i + 1))

                def bias_and_max(t):
                    n, near = (t + 1) * P, min((t + 1) * P, 2 * P)
                    dve.wait_ge(sc_done, TT * i + t + 1)
                    bank = ps_s[t % 2]
                    dve.scalar_tensor_tensor(prob[:, t, n - near:n], bank[:, n - near:n], SCALE,
                                             band[:, 2 * P - near:], ALU.mult, ALU.add)
                    if n > near:
                        dve.tensor_scalar(prob[:, t, 0:n - near], bank[:, 0:n - near], SCALE, band[:, 0:1],
                                          ALU.mult, ALU.add)
                    dve.drain()
                    dve.tensor_reduce(row_max[:, t:t + 1], prob[:, t, 0:n], AX.X, ALU.max)
                    dve.drain()
                    dve.tensor_scalar(neg_max[:, t:t + 1], row_max[:, t:t + 1], -1.0, None,
                                      ALU.mult).then_inc(max_made, 1)

                def divide(t):
                    n = (t + 1) * P
                    dve.wait_ge(exp_made, TT * i + t + 1)
                    dve.reciprocal(row_rec[:, t:t + 1], row_sum[:, t:t + 1])
                    dve.drain()
                    dve.tensor_scalar(prob[:, t, 0:n], prob[:, t, 0:n], row_rec[:, t:t + 1], None,
                                      ALU.mult).then_inc(prob_made, 1)

                bias_and_max(0)
                bias_and_max(1)
                divide(0)
                divide(1)
                bias_and_max(2)
                bias_and_max(3)
                divide(2)
                divide(3)

            dve.wait_ge(split_hi_made, 1)
            tt(ys_lo[:, :, :], y_ssm[:, :, :], ys_hi[:, :, :].bitcast(F32), ALU.subtract).then_inc(split_lo_made, 1)
            dve.wait_ge(split_hi_made, 2)
            tt(ya_lo[:, :, :], y_attn[:, :, :], ya_hi[:, :, :].bitcast(F32), ALU.subtract).then_inc(split_lo_made, 1)

            def split(src, hi, lo):
                dve.tensor_copy(hi, src)
                dve.drain()
                return tt(lo, src, hi.bitcast(F32), ALU.subtract)

            with dve.Fori(0, WC // 2) as j:
                for s in range(2):
                    m = 2 * j + s
                    dve.wait_ge(evac, m + 3)
                    at = bass.ds(m, 1)
                    y3 = glu_y[:, :].unsqueeze(1)
                    tt(y3, y_ssm[:, at, :], glu_s[s][:, :].unsqueeze(1), ALU.mult)
                    dve.drain()
                    split(y3, y2_hi[:, at, :], y2_lo[:, at, :]).then_inc(glu_made, 1)
                    dve.drain()

            with dve.Fori(0, DC // 2) as j:
                for s in range(2):
                    d = 2 * j + s
                    dve.wait_ge(sig_made, d + 1)
                    dve.wait_ge(blk_done, BLK_UP + 2 * d + 1)
                    tt(up_a[:, :], ps_p[0][:, :], gates[s][:, 0, :], ALU.mult).then_inc(evac, 1)
                    dve.wait_ge(blk_done, BLK_UP + 2 * d + 2)
                    tt(up_s[:, :], ps_p[1][:, :], gates[s][:, 1, :], ALU.mult).then_inc(evac, 1)
                    dve.drain()
                    tt(up_m[:, :], up_a[:, :], up_s[:, :], ALU.add)
                    dve.drain()
                    at = bass.ds(d, 1)
                    split(up_m[:, :].unsqueeze(1), m_hi[:, at, :], m_lo[:, at, :]).then_inc(merged, 1)
                    dve.drain()

            dve.wait_ge(res_landed, 16 * TT)
            with dve.Fori(0, DC // 2) as j:
                for s in range(2):
                    o = 2 * j + s
                    dve.wait_ge(mt_turned, o + 3)
                    at = bass.ds(o * P, P)
                    dve.scalar_tensor_tensor(res[:, :, at], res[:, :, at], ALPHA,
                                             ps_t[s][:, :].rearrange("p (t n) -> p t n", t=TT), ALU.mult,
                                             ALU.add).then_inc(mt_used, 1)
            dve.drain()
            statistics(res, 2, None)
            dve.wait_ge(ln1_landed, 32)
            gain_bias(res, ln_g, ln_b, 1)
            turned_lo(h1_lo, h1_hi, 1)
            dve.wait_ge(pw_evac, 16)
            dve.tensor_reduce(sq_tot[:, :], sq_sum[:, :, :], AX.X, ALU.add)
            dve.drain()
            dve.tensor_scalar(sq_tot[:, :], sq_tot[:, :], 1.0 / D, EPS, ALU.mult, ALU.add).then_inc(ms_ready, 1)
            dve.wait_ge(rms_ready, 1)
            dve.reciprocal(sq_rec[:, :], sq_tot[:, :])
            dve.drain()
            dve.wait_ge(emb_g_landed, 16)
            for t in range(TT):
                dve.scalar_tensor_tensor(emb[:, t, :], emb[:, t, :], sq_rec[:, t:t + 1], emb_g[:, :], ALU.mult,
                                         ALU.mult)
            dve.drain()

            def top16(src, other, vals, idx, tiles, after=None):
                for t in tiles:
                    dve.max(vals[:, t, 0:8], src(t))
                dve.drain()
                for t in tiles:
                    dve.max_index(idx[:, t, 0:8], vals[:, t, 0:8], src(t))
                for t in tiles:
                    last = dve.match_replace(other(t), vals[:, t, 0:8], src(t), -3.0e38)
                if after is not None:
                    last.then_inc(after, 1)
                dve.drain()
                for t in tiles:
                    dve.max(vals[:, t, 8:16], other(t))
                dve.drain()
                for t in tiles:
                    dve.max_index(idx[:, t, 8:16], vals[:, t, 8:16], other(t))
                dve.drain()

            with dve.Fori(0, RH) as j:
                for s in range(2):
                    o = 2 * j + s
                    dve.wait_ge(mt_turned, N_OUT + o + 3)
                    dve.memset(gate_sum[:, 0:1], 0.0)
                    top16(lambda t: ps_t[s][:, t * P:(t + 1) * P], lambda t: rest[:, t, :], top_v, top_i, range(TT),
                          mt_used)
                    at = bass.ds(o, 1)
                    dve.tensor_copy(v_all[:, :, at, :], top_v[:, :, :].unsqueeze(2))
                    dve.tensor_copy(i_all[:, :, at, :], top_i[:, :, :].unsqueeze(2))
                    dve.drain()

            with dve.Fori(0, RH) as j:
                def embed(s):
                    o = 2 * j + s
                    dve.wait_ge(mt_turned, N_OUT + N_Q + o + 3)
                    at = bass.ds(o * P, P)
                    tt(emb_add[:, :, :], ps_t[s][:, :].rearrange("p (t n) -> p t n", t=TT), emb[:, :, at],
                       ALU.mult).then_inc(mt_used, 1)
                    dve.drain()
                    dve.scalar_tensor_tensor(res[:, :, at], res[:, :, at], ALPHA, emb_add[:, :, :], ALU.mult,
                                             ALU.add)
                    dve.drain()

                wide = [P, TT, TOPK, TOPK]
                one, two = bass.ds(2 * j, 1), bass.ds(2 * j + 1, 1)
                tt(cand[:, :, :, :],
                   v_all[:, :, one, :].rearrange("p t a k -> p t (a k)").unsqueeze(3).to_broadcast(wide),
                   v_all[:, :, two, :].to_broadcast(wide), ALU.add)
                dve.drain()

                def best(tiles):
                    top16(lambda t: cand[:, t, :, :].rearrange("p a b -> p (a b)"), lambda t: cand_rest[:, t, :],
                          top_v, top_i, tiles)

                embed(0)
                best(range(0, 2))
                embed(1)
                best(range(2, 4))
                at = bass.ds(j * TOPK, TOPK)
                tt(sel_g[:, :, at], top_v[:, :, :], top_v[:, :, 0:1].to_broadcast([P, TT, TOPK]), ALU.subtract)
                dve.tensor_scalar(pos_a[:, :, :], top_i[:, :, :], 4, None, ALU.logical_shift_right)
                dve.tensor_scalar(pos_b[:, :, :], top_i[:, :, :], 15, None, ALU.bitwise_and)
                dve.drain()
                dve.tensor_copy(pos_af[:, :, :], pos_a[:, :, :])
                dve.tensor_copy(pos_bf[:, :, :], pos_b[:, :, :])
                dve.drain()
                flat = [P, TT * TOPK, TOPK]
                for eq, pos in ((eq_a, pos_af), (eq_b, pos_bf)):
                    tt(eq[:, :, :, :].rearrange("p t k a -> p (t k) a"),
                       iota[:, 0:TOPK].unsqueeze(1).to_broadcast(flat),
                       pos[:, :, :].rearrange("p t k -> p (t k)").unsqueeze(2).to_broadcast(flat), ALU.is_equal)
                dve.drain()
                for eq, half in ((eq_a, one), (eq_b, two)):
                    tt(eq[:, :, :, :], eq[:, :, :, :], i_all[:, :, half, :].to_broadcast(wide), ALU.mult)
                dve.drain()
                for eq, sel in ((eq_a, sel_i), (eq_b, sel_j)):
                    dve.tensor_reduce(sel[:, :, at], eq[:, :, :, :], AX.X, ALU.add)
                dve.drain()
            dve.sem_inc(picks_made, 1)
            dve.wait_ge(exps_made, 1)
            g4 = sel_g[:, :, :].rearrange("p t (r k) -> p (t r) k", k=TOPK)
            dve.tensor_reduce(gate_sum[:, :], g4, AX.X, ALU.add)
            dve.drain()
            dve.reciprocal(gate_rec[:, :], gate_sum[:, :])
            dve.drain()
            tt(g4, g4, gate_rec[:, :].unsqueeze(2).to_broadcast([P, TT * RH, TOPK]), ALU.mult).then_inc(gates_made, 1)
            dve.wait_ge(pick_gh_made, 1)
            tt(pick_gl[:, :], ps_t[0][:, :], pick_gh[:, :].bitcast(F32), ALU.subtract)
            dve.drain()

            with dve.Fori(0, HOT_ITER) as j:
                at = bass.ds(4 * HOT * j, 4 * HOT)
                for z, src in enumerate((pick_i[:, at], pick_j[:, at], pick_gh[:, at].bitcast(F32), pick_gl[:, at])):
                    dve.tensor_copy(cols[:, z, :], src)
                dve.drain()
                for s in range(4):
                    for k in range(HOT):
                        c = HOT * s + k
                        dve.tensor_scalar(hot_j[:, k, :], iota[:, :], cols[:, 1, c:c + 1], None, ALU.is_equal)
                        for z in range(2):
                            last = dve.tensor_scalar(hot_g[:, k, z, :], iota[:, :], cols[:, 0, c:c + 1],
                                                     cols[:, 2 + z, c:c + 1], ALU.is_equal, ALU.mult)
                    last.then_inc(hot_made, 1)
                    dve.wait_ge(hot_moved, 4 * j + s + 1)
                    for m in range(HOT // 2):
                        last = tt(hot_out(s, m), hot_out(s, m), hot_in(m)[:, 1], ALU.add)
                    if s % 2 == 1:
                        last.then_inc(hot_evac, 1)
                    dve.drain()

            def weights_of(sbn, k, landed):
                dve.wait_ge(aux_landed[k], landed)
                tt(ew[:, :, :], act_in[k][:, :, :], gate_in[k][:, :, :].rearrange("p t i -> p i t"), ALU.mult)
                dve.drain()
                if not (isinstance(sbn, int) and sbn == 0):
                    dve.wait_ge(v_done, 16 * (sbn - 1) + 1)
                split(ew[:, :, :], ew_hi[k][:, :, :], ew_lo[k][:, :, :]).then_inc(ew_made, 1)
                dve.drain()

            weights_of(0, 0, 32)

            def expert_pair(j, last):
                for k in range(2):
                    for c in range(4):
                        if c == 3 and not (last and k == 1):
                            weights_of(2 * j + k + 1, (k + 1) % 2, 32 * (j + 1 + k))
                        for t in range(TT):
                            dve.wait_ge(v_done, 4 * (8 * j + 4 * k + c) + t + 2)
                            part = res[:, t, c * 512:(c + 1) * 512]
                            tt(part, part, ps[4 * ((c + 1) % 2) + t][:, :], ALU.add).then_inc(v_added, 1)
                    dve.drain()

            with dve.Fori(0, SB // 2 - 1) as j:
                expert_pair(j, False)
            expert_pair(SB // 2 - 1, True)
            statistics(res, 3, None)
            dve.wait_ge(ln2_landed, 32)
            gain_bias(res, ln2_g, ln2_b, 2)


def _blocks(a, chunks):
    return a.reshape(chunks, P, a.shape[1] // P, P).transpose(2, 1, 0, 3)


def _slabs(i):
    order = [b for h in range(HEADS)
             for b in (24 + h, h, 8 + h, 16 + h, 32 + 4 * h, 33 + 4 * h, 34 + 4 * h, 35 + 4 * h)]
    parts = [_blocks(i["w_in"][0], DC)[order].reshape(N_IN, P, SL)]
    glu = _blocks(i["w_ssm_glu"][0], WC).reshape(N_GLU, 2, P, HALF).transpose(0, 2, 1, 3)
    parts.append(glu.reshape(N_GLU, P, SL))
    up = np.stack([_blocks(i["w_attn_up"][0], WC), _blocks(i["w_ssm_up"][0], WC)], 1)
    parts.append(up.transpose(0, 2, 1, 3, 4).reshape(N_UP, P, SL))
    for name in ("w_mix_out", "w_peer_q", "ple_w_gate"):
        parts.append(_blocks(i[name][0], DC).reshape(DC, P, SL))
    parts.append(i["peer_u"][0].reshape(EB, P, DC, P).transpose(0, 3, 2, 1).reshape(N_U, P, SL))
    parts.append(i["peer_v"][0].reshape(SB, 4, P, 4, 512).transpose(0, 3, 2, 1, 4).reshape(N_V, P, SL))
    return np.concatenate(parts, 0)


def _states(a):
    return a.reshape(QN, 2, ST).transpose(1, 2, 0).reshape(P, QN)


def kernel(**inputs):
    import concourse.bacc as bacc
    from concourse.bass_utils import run_bass_kernel_spmd

    i = {k: np.asarray(v) for k, v in inputs.items()}
    rel = i["attn_rel_bias"][0][:, ::-1]
    b_c = np.stack([i["ssm_b_re"][0], i["ssm_b_im"][0]]).reshape(2, QN, 2, ST, GCH)
    c_c = np.stack([i["ssm_c_re"][0], i["ssm_c_im"][0]]).reshape(2, HEADS, CB_Q, 2, GCH, ST)
    names = ("ln_in_g", "ln_in_b", "ln1_g", "ln1_b", "ple_norm_g", "ln2_g", "ln2_b")
    arrays = {
        "x": i["x"][0],
        "p_t": i["p"][0, 0].T.reshape(2, P, S).transpose(1, 0, 2),
        "vecs": np.stack([i[n].reshape(D) for n in names]),
        "weights": _slabs(i),
        "band_ext": np.concatenate([np.repeat(rel[:, :1], P - 1, 1), rel], 1),
        "lam_re": _states(i["ssm_lam_re"][0]),
        "lam_im": _states(i["ssm_lam_im"][0]),
        "log_dt": i["ssm_log_dt"][0].reshape(QN, 2).T,
        "b_in": b_c.transpose(2, 3, 0, 1, 4).reshape(P, 2, QN, GCH),
        "c_in": c_c.transpose(1, 3, 5, 0, 2, 4).reshape(HEADS, P, 2, CB_Q, GCH),
        "d_skip": i["ssm_d"].reshape(W2),
        "keys_t": i["peer_sub_keys"][0].reshape(2 * RH, NK, P).transpose(2, 0, 1),
        "ple_w": i["ple_w_in"][0].reshape(2, P, D).transpose(1, 0, 2),
    }
    arrays = {f"in_{k}": np.ascontiguousarray(v) for k, v in arrays.items()}
    nc = bacc.Bacc("TRN2", target_bir_lowering=False, num_devices=1, dynamic_dma_scratch_size=1024)
    args = {k[3:]: nc.dram_tensor(k, v.shape, F32, kind="ExternalInput").ap() for k, v in arrays.items()}
    out = nc.dram_tensor("out_dram", (S, D), F32, kind="ExternalOutput").ap()
    build_trunk(nc, out=out, **args)
    r = run_bass_kernel_spmd(nc, [arrays], core_ids=[0])
    return r.results[0]["out_dram"].reshape(1, S, D)
```

```python
import concourse.bass as bass
import numpy as np
from concourse import mybir

F32 = mybir.dt.float32
F32R = mybir.dt.float32r
U32 = mybir.dt.uint32
ALU = mybir.AluOpType
ACT = mybir.ActivationFunctionType
AX = mybir.AxisListType

P = 128
S = 512
D = 2048
TT = S // P
DC = D // P
HEADS, DH = 8, 128
W2 = 1024
WC = W2 // P
GROUPS, GCH, ST = 64, 16, 64
LC = 8
NC = S // LC
CB_G = 8
CB_Q = CB_G // 2
QN = GROUPS // 2
RH, NK, TOPK = 8, 128, 16
EB = NK
SB = EB // 4
HOT = 8
HOT_FROM = 2
HOT_ITER = S // (4 * HOT)
PLE = 256
POOL_TILES = ((), (1, 2), (0, 1, 2))
EPS = 1e-5
ALPHA = 2.0 ** 0.25
SCALE = DH ** -0.5

SL = 2048
HALF = SL // 2
N_IN = 64
N_GLU = 4
N_UP = 16
N_OUT, N_Q, N_GATE = 16, 16, 16
N_U, N_V = 128, 128
AT_GLU = N_IN
AT_UP = AT_GLU + N_GLU
AT_OUT = AT_UP + N_UP
AT_Q = AT_OUT + N_OUT
AT_GATE = AT_Q + N_Q
AT_U = AT_GATE + N_GATE
AT_V = AT_U + N_U
N_SLABS = AT_V + N_V
BLK_GLU = N_IN + 1
BLK_UP = BLK_GLU + 2 * N_GLU
BLK_OUT = BLK_UP + 2 * N_UP
BLK_Q = BLK_OUT + N_OUT
BLK_GATE = BLK_Q + N_Q
BLK_U = BLK_GATE + N_GATE
BLK_V = BLK_U + N_U

TWO_PI_1 = 6.28125
TWO_PI_2 = float(np.round((2 * np.pi - TWO_PI_1) * 2.0**19) / 2.0**19)
TWO_PI_3 = float(2 * np.pi - TWO_PI_1 - TWO_PI_2)
ROUND = 1.5 * 2.0**23
PI_F32 = 3.1415925


def fact(n):
    return float(np.prod(np.arange(1, n + 1, dtype=np.float64)))


def cmul(eng, o_re, o_im, a, b, ta, tb, minus_im=False):
    eng.tensor_tensor(ta, a[0], b[0], ALU.mult)
    eng.tensor_tensor(tb, a[1], b[1], ALU.mult)
    eng.drain()
    eng.tensor_tensor(o_re, ta, tb, ALU.subtract)
    eng.drain()
    eng.tensor_tensor(ta, a[0], b[1], ALU.mult)
    eng.tensor_tensor(tb, a[1], b[0], ALU.mult)
    eng.drain()
    if minus_im:
        last = eng.scalar_tensor_tensor(o_im, ta, -1.0, tb, ALU.mult, ALU.subtract)
    else:
        last = eng.tensor_tensor(o_im, ta, tb, ALU.add)
    eng.drain()
    return last


def build_trunk(nc, x, p_t, vecs, weights, band_ext, lam_re, lam_im, log_dt, b_in, c_in, d_skip,
                keys_t, ple_w, out):
    kb = 1024
    base = 1152
    ring_at, a_at = base, base + 48 * kb
    c_at = a_at + 64 * kb
    k_at = c_at + 32 * kb
    w_at = k_at + 2 * kb

    def sb(name, shape, at, dt=F32):
        return nc.alloc_sbuf_tensor_at(name, shape, dt, offset=int(at))

    def w(name, shape, at_kb, dt=F32):
        return sb(name, shape, w_at + at_kb * kb, dt)

    raw = [sb(f"raw{i}", [P, SL], ring_at + 8 * kb * i) for i in range(2)]
    whi = [sb(f"whi{i}", [P, SL], ring_at + 16 * kb + 8 * kb * i, F32R) for i in range(2)]
    wlo = [sb(f"wlo{i}", [P, SL], ring_at + 32 * kb + 8 * kb * i, F32R) for i in range(2)]
    h0_hi = sb("h0_hi", [P, DC, S], a_at, F32R)
    h0_lo = sb("h0_lo", [P, DC, S], a_at + 32 * kb, F32R)
    xt = sb("xt", [P, TT, D], c_at)
    y_attn = sb("y_attn", [P, WC, S], c_at)
    y_ssm = sb("y_ssm", [P, WC, S], c_at + 16 * kb)
    ident = sb("ident", [P, P], k_at)
    iota = sb("iota", [P, P], k_at + 512)
    stat = sb("stat", [P, TT, 4, 6], k_at + 1024)
    mv = sb("mv", [P, TT, 2], k_at + 1408)
    std = sb("std", [P, TT], k_at + 1440)
    rstd = sb("rstd", [P, TT], k_at + 1472)
    shift = sb("shift", [P, TT], k_at + 1504)
    row_max = sb("row_max", [P, TT], k_at + 1536)
    neg_max = sb("neg_max", [P, TT], k_at + 1568)
    row_sum = sb("row_sum", [P, TT], k_at + 1600)
    row_rec = sb("row_rec", [P, TT], k_at + 1632)
    g_in = w("g_in", [P, D], 0)
    b_ln_in = w("b_ln_in", [P, D], 8)
    q_h = w("q_h", [P, S], 0)
    k_h = w("k_h", [P, S], 2)
    v_h = w("v_h", [P, S], 4)
    v_keys = w("v_keys", [P, TT, DH], 6)
    prob = w("prob", [P, TT, S], 8)
    u_sc = w("u_sc", [P, CB_G, NC], 16)
    g_out = [w(f"g_out{i}", [P, S], 18 + 2 * i) for i in range(2)]
    toep = w("toep", [P, CB_G, P], 22)
    y_sc = w("y_sc", [P, CB_G, NC], 26)
    y_cs = w("y_cs", [P, LC, NC], 28)
    t1 = w("t1", [P, 640], 30)
    t2 = w("t2", [P, 640], 32.5)
    in_map = w("in_map", [P, 2, CB_Q, P], 35)
    prob_t = w("prob_t", [P, TT, S], 39)
    e_tab = w("e_tab", [P, 2, CB_Q, LC, GCH], 39)
    u_cs = w("u_cs", [P, LC, NC], 43)
    f_tab = w("f_tab", [P, 2, CB_Q, LC + 1, GCH], 47)
    h_pair = w("h_pair", [P, 2, CB_Q, 2, NC], 39)
    h_st = w("h_st", [P, 2, CB_Q, NC + 1], 51.5)
    k_tab = w("k_tab", [2 * GCH, CB_Q, P], 54)
    bb_pair = w("bb_pair", [P, 2, CB_Q, 2, GCH], 56)
    pow_up = w("pow_up", [P, 2, QN, LC + 1], 58)
    pow_dn = w("pow_dn", [P, 2, QN, LC + 1], 60.5)
    lev = w("lev", [P, 2, QN, 6], 63)
    bb = w("bb", [P, 2, QN, GCH], 64.5)
    c_s = w("c_s", [P, 2, CB_Q, GCH], 68.5)
    bb_s = w("bb_s", [P, 2, CB_Q, GCH], 69)
    pow_up_s = w("pow_up_s", [P, 2, CB_Q, LC + 1], 69.5)
    pow_dn_s = w("pow_dn_s", [P, 2, CB_Q, LC + 1], 70)
    lev_s = w("lev_s", [P, 2, CB_Q, 6], 70.5)
    band = w("band", [P, 2 * P], 71)
    d_bc = w("d_bc", [2 * GCH, W2], 72)
    d_diag = w("d_diag", [2 * GCH, CB_Q, 2, GCH], 76)
    prm = w("prm", [P, 20, QN], 39)
    b_raw = w("b_raw", [P, 2, QN, GCH], 41.5)

    ya_hi = sb("ya_hi", [P, WC, S], a_at, F32R)
    ya_lo = sb("ya_lo", [P, WC, S], a_at + 16 * kb, F32R)
    y2_hi = sb("y2_hi", [P, WC, S], a_at + 32 * kb, F32R)
    y2_lo = sb("y2_lo", [P, WC, S], a_at + 48 * kb, F32R)
    res = sb("res", [P, TT, D], a_at)
    emb = sb("emb", [P, TT, D], a_at + 32 * kb)
    gate_st = [sb(f"gate_st{i}", [P, SB, 16, 4], a_at + (32 + 8 * i) * kb) for i in range(2)]
    hot_j = sb("hot_j", [P, HOT, P], a_at + 52 * kb, F32R)
    hot_g = sb("hot_g", [P, HOT, 2, P], a_at + 56 * kb, F32R)
    ys_hi = w("ys_hi", [P, WC, S], 0, F32R)
    ys_lo = w("ys_lo", [P, WC, S], 16, F32R)
    glu_s = [w(f"glu_s{i}", [P, S], 32 + 2 * i) for i in range(2)]
    glu_y = w("glu_y", [P, S], 36)
    m_hi = w("m_hi", [P, DC, S], 0, F32R)
    m_lo = w("m_lo", [P, DC, S], 32, F32R)
    h1_hi = w("h1_hi", [P, DC, S], 0, F32R)
    h1_lo = w("h1_lo", [P, DC, S], 32, F32R)
    up_a = w("up_a", [P, S], 64)
    up_s = w("up_s", [P, S], 66)
    up_m = w("up_m", [P, S], 68)
    p_sb = w("p_sb", [P, 2, S], 64)
    junk = w("junk", [P, 1024], 64)
    emb_add = w("emb_add", [P, TT, P], 64)
    mt = [w(f"mt{i}", [P, S], 70 + 2 * i) for i in range(2)]
    top_v = w("top_v", [P, TT, TOPK], 74)
    top_i = w("top_i", [P, TT, TOPK], 74.25, U32)
    pos_a = w("pos_a", [P, TT, TOPK], 74.5, U32)
    pos_b = w("pos_b", [P, TT, TOPK], 74.75, U32)
    pos_af = w("pos_af", [P, TT, TOPK], 75)
    pos_bf = w("pos_bf", [P, TT, TOPK], 75.25)
    sq_sum = w("sq_sum", [P, 2 * TT], 75.5)
    sq_tot = w("sq_tot", [P, TT], 75.625)
    sq_rec = w("sq_rec", [P, TT], 75.75)
    gate_sum = w("gate_sum", [P, TT * RH], 75.875)
    gate_rec = w("gate_rec", [P, TT * RH], 76)
    gates = [sb(f"gates{i}", [P, 2, S], c_at + 4 * kb * i) for i in range(2)]
    ln_g = sb("ln_g", [P, D], c_at)
    ln_b = sb("ln_b", [P, D], c_at + 8 * kb)
    pw_sb = sb("pw_sb", [P, 2, D], c_at + 16 * kb)
    emb_g = sb("emb_g", [P, D], c_at)
    keys = sb("keys", [P, 2 * RH, NK], c_at + 8 * kb)
    v_all = sb("v_all", [P, TT, 2 * RH, TOPK], c_at + 16 * kb)
    i_all = sb("i_all", [P, TT, 2 * RH, TOPK], c_at + 20 * kb)
    rest = sb("rest", [P, TT, NK], c_at + 24 * kb)
    sel_i = sb("sel_i", [P, TT, P], c_at + 26 * kb)
    sel_j = sb("sel_j", [P, TT, P], c_at + 28 * kb)
    sel_g = sb("sel_g", [P, TT, P], c_at + 30 * kb)
    cand = sb("cand", [P, TT, TOPK, TOPK], c_at)
    cand_rest = sb("cand_rest", [P, TT, TOPK * TOPK], c_at + 4 * kb)
    eq_a = sb("eq_a", [P, TT, TOPK, TOPK], c_at + 8 * kb)
    eq_b = sb("eq_b", [P, TT, TOPK, TOPK], c_at + 12 * kb)
    pick_i = sb("pick_i", [P, S], c_at)
    pick_j = sb("pick_j", [P, S], c_at + 2 * kb)
    pick_gh = sb("pick_gh", [P, S], c_at + 4 * kb, F32R)
    pick_gl = sb("pick_gl", [P, S], c_at + 6 * kb)
    cols = sb("cols", [P, 4, 4 * HOT], c_at + 8 * kb)
    act_in = [sb("act_in0", [P, 4, S], c_at), w("act_in1", [P, 4, S], 0)]
    gate_in = [sb("gate_in0", [P, S, 4], c_at + 8 * kb), w("gate_in1", [P, S, 4], 8)]
    ew_hi = [sb("ew_hi0", [P, 4, S], c_at + 16 * kb, F32R), w("ew_hi1", [P, 4, S], 16, F32R)]
    ew_lo = [sb("ew_lo0", [P, 4, S], c_at + 24 * kb, F32R), w("ew_lo1", [P, 4, S], 24, F32R)]
    ew = sb("ew", [P, 4, S], a_at + 56 * kb)
    ln2_g = w("ln2_g", [P, D], 32)
    ln2_b = w("ln2_b", [P, D], 40)

    ps = [nc.alloc_psum_tensor(f"bank{i}", [P, S], F32) for i in range(8)]
    ps_p, ps_s, ps_t, ps_x, ps_y = ps[0:2], ps[2:4], ps[4:6], ps[6], ps[7]
    ps_pt = [ps_t[0], ps_t[1], ps_s[0], ps_s[1]]

    def hot_in(m):
        return ps[2 + m][:, :].rearrange("p (t z b i) -> p z b t i", t=2, z=2, i=4)

    def hot_out(s, m):
        at = HOT * (s % 2) + 2 * m
        return gate_st[s // 2][:, :, at:at + 2, :]

    def dram(name, shape):
        return nc.dram_tensor(name, shape, F32, kind="Internal").ap()

    h0_d = dram("h0_d", [TT, P, D])
    gate_d = dram("gate_d", [2 * DC, P, S])
    u_d = dram("u_d", [P, LC, NC])
    k_d = dram("k_d", [GCH, CB_G, (2 * LC - 1) * GCH])
    act_d = dram("act_d", [SB, P, 4, S])
    pick_d = dram("pick_d", [SB, P, S * 4])
    band_d = dram("band_d", [HEADS, P, 2 * P])
    y_d = dram("y_d", [P, CB_G, NC])

    sem = {}

    def sm(name):
        sem[name] = nc.alloc_semaphore(name)
        return sem[name]

    raw_landed = [sm("raw_landed0"), sm("raw_landed1")]
    hi_made, lo_made, blk_done, evac = sm("hi_made"), sm("lo_made"), sm("blk_done"), sm("evac")
    x_landed = [sm(f"x_landed{i}") for i in range(TT)]
    ln_in_landed, ident_made = sm("ln_in_landed"), sm("ident_made")
    var_ready, std_ready, rstd_ready = sm("var_ready"), sm("std_ready"), sm("rstd_ready")
    xn_ready, h_ready, turned = sm("xn_ready"), sm("h_ready"), sm("turned")
    gained, pool_h_ready = sm("gained"), sm("pool_h_ready")
    turn_hi, turn_lo, h0_stored = sm("turn_hi"), sm("turn_lo"), sm("h0_stored")
    prm_landed, dt_ready, prm_ready = sm("prm_landed"), sm("dt_ready"), sm("prm_ready")
    den_ready, b_landed = sm("den_ready"), sm("b_landed")
    c_landed, ef_made, band_landed = sm("c_landed"), sm("ef_made"), sm("band_landed")
    u_stored, u_landed = sm("u_stored"), sm("u_landed")
    e_turned, in_map_made, k_done, k_made = sm("e_turned"), sm("in_map_made"), sm("k_done"), sm("k_made")
    k_zeroed, k_stored, toep_landed = sm("k_zeroed"), sm("k_stored"), sm("toep_landed")
    bu_done, h_filled, scanned, y_done = sm("bu_done"), sm("h_filled"), sm("scanned"), sm("y_done")
    y_made, y_stored, y_landed = sm("y_made"), sm("y_stored"), sm("y_landed")
    qkv_made, v_turned, v_made = sm("qkv_made"), sm("v_turned"), sm("v_made")
    sc_done, max_made, exp_made, prob_made = sm("sc_done"), sm("max_made"), sm("exp_made"), sm("prob_made")
    pt_done, pt_made, pv_done = sm("pt_done"), sm("pt_made"), sm("pv_done")
    g_stored = [sm("g_stored0"), sm("g_stored1")]
    band_laid = sm("band_laid")
    split_hi_made, split_lo_made, glu_made = sm("split_hi_made"), sm("split_lo_made"), sm("glu_made")
    gates_landed = [sm("gates_landed0"), sm("gates_landed1")]
    sig_made, merged, res_landed = sm("sig_made"), sm("merged"), sm("res_landed")
    mt_turned, mt_used = sm("mt_turned"), sm("mt_used")
    ple_landed, ln1_landed, pw_done, pw_evac = sm("ple_landed"), sm("ln1_landed"), sm("pw_done"), sm("pw_evac")
    keys_landed, emb_g_landed = sm("keys_landed"), sm("emb_g_landed")
    sq_made, ms_ready, rms_ready = sm("sq_made"), sm("ms_ready"), sm("rms_ready")
    picks_made, exps_made, gates_made, picks_turned = sm("picks_made"), sm("exps_made"), sm("gates_made"), sm("picks_turned")
    pick_gh_made = sm("pick_gh_made")
    hot_made, hot_done, hot_moved, hot_evac = sm("hot_made"), sm("hot_done"), sm("hot_moved"), sm("hot_evac")
    pick_stored = [sm("pick_stored0"), sm("pick_stored1")]
    act_stored = [sm("act_stored0"), sm("act_stored1")]
    aux_landed = [sm("aux_landed0"), sm("aux_landed1")]
    ew_made, v_done, v_added = sm("ew_made"), sm("v_done"), sm("v_added")
    ln2_landed, out_stored = sm("ln2_landed"), sm("out_stored")
    branch_made = sm("branch_made")

    def pool_count(first):
        return sum(len(POOL_TILES[n]) for n in range(first))

    def wait_tile(engine, first, t):
        if first == 0:
            engine.wait_ge(h_ready, t + 1)
        elif t in POOL_TILES[first]:
            engine.wait_ge(pool_h_ready, pool_count(first) + POOL_TILES[first].index(t) + 1)
        else:
            others = [u for u in range(TT) if u not in POOL_TILES[first]]
            engine.wait_ge(h_ready, TT * first - pool_count(first) + others.index(t) + 1)

    block = nc.Block()
    with block:

        @block.sync
        def _(sp):
            def load_slab(n, slot):
                sp.wait_ge(lo_made, 2 * n + 1)
                sp.dma_start(raw[slot][:, :], weights[bass.ds(n, 1), :, :].rearrange("a p n -> (a p) n")
                             ).then_inc(raw_landed[slot], 16)

            sp.dma_start(prm[:, 0, :], lam_re).then_inc(prm_landed, 16)
            sp.dma_start(prm[:, 1, :], lam_im).then_inc(prm_landed, 16)
            for r in range(2):
                sp.dma_start(prm[ST * r:ST * (r + 1), 2, :], log_dt[r].partition_broadcast(ST)
                             ).then_inc(prm_landed, 16)

            def load_x(t):
                sp.dma_start(xt[:, t, :], x[t * P:(t + 1) * P, :]).then_inc(x_landed[t], 16)

            load_x(0)
            load_x(1)
            sp.dma_start(g_in[:, :], vecs[0:1, :].rearrange('a d -> (a d)').partition_broadcast(P)).then_inc(ln_in_landed, 16)
            sp.dma_start(b_ln_in[:, :], vecs[1:2, :].rearrange('a d -> (a d)').partition_broadcast(P)).then_inc(ln_in_landed, 16)
            load_x(2)
            load_x(3)
            sp.dma_start(b_raw[:, :, :, :], b_in).then_inc(b_landed, 16)
            sp.dma_start(d_bc[:, :], d_skip.partition_broadcast(2 * GCH)).then_inc(b_landed, 16)
            load_slab(0, 0)
            load_slab(1, 1)
            sp.dma_start(band_d, bass.AP(band_ext.tensor, 127, [[384, HEADS], [-1, P], [1, 2 * P]])
                         ).then_inc(band_laid, 16)
            sp.wait_ge(band_laid, 16)

            with sp.Fori(0, HEADS) as i:
                sp.wait_ge(ef_made, i + 1)
                sp.dma_start(c_s[:, :, :, :], c_in[bass.ds(i, 1)].rearrange("a p r q c -> (a p) r q c")
                             ).then_inc(c_landed, 16)
                for b in range(8):
                    load_slab(8 * i + b + 2, b % 2)
                    if b == 1:
                        sp.wait_ge(max_made, TT * i + 1)
                        bias = band_d[bass.ds(i, 1)].rearrange("a p n -> (a p) n")
                        sp.dma_start(band[:, 0:192], bias[:, 0:192]).then_inc(band_landed, 16)
                        sp.dma_start(band[64:P, 192:256], bias[64:P, 192:256]).then_inc(band_landed, 16)
                    if b == 2:
                        sp.wait_ge(u_stored, 16 * (i + 1))
                        for s in range(LC):
                            sp.dma_start(u_sc[GCH * s:GCH * (s + 1), :, :],
                                         u_d.rearrange("(g c) s n -> s c g n", c=GCH)[s]).then_inc(u_landed, 16)
                    if b == 4:
                        sp.wait_ge(k_zeroed, 33)
                        sp.wait_ge(k_stored, 32 * (i + 1) + 16)
                        for s in range(LC):
                            sp.dma_start(toep[GCH * s:GCH * (s + 1), :, :],
                                         k_d[:, :, (LC - 1 - s) * GCH:(LC - 1 - s) * GCH + P]
                                         ).then_inc(toep_landed, 16)
                    if b == 7:
                        sp.wait_ge(y_stored, 16 * (i + 1))
                        for g in range(CB_G):
                            sp.dma_start(y_cs[GCH * g:GCH * (g + 1), :, :],
                                         y_d.rearrange("(s c) g n -> g c s n", c=GCH)[g]).then_inc(y_landed, 16)

            def row(j):
                return vecs[j:j + 1, :].rearrange("a d -> (a d)").partition_broadcast(P)

            with sp.Fori(AT_GLU // 2 + 1, AT_UP // 2) as j:
                for s in range(2):
                    load_slab(2 * j + s, s)
            with sp.Fori(AT_UP // 2, AT_OUT // 2) as j:
                for s in range(2):
                    load_slab(2 * j + s, s)
            with sp.Fori(AT_OUT // 2, AT_Q // 2 - 2) as j:
                for s in range(2):
                    load_slab(2 * j + s, s)
            sp.wait_ge(merged, DC + 1)
            sp.dma_start(ln_g[:, :], row(2)).then_inc(ln1_landed, 16)
            sp.dma_start(ln_b[:, :], row(3)).then_inc(ln1_landed, 16)
            sp.dma_start(pw_sb[:, :, :], ple_w).then_inc(ple_landed, 16)
            sp.dma_start(p_sb[:, :, :], p_t).then_inc(ple_landed, 16)
            with sp.Fori(AT_Q // 2 - 2, AT_Q // 2 + 1) as j:
                for s in range(2):
                    load_slab(2 * j + s, s)
            for t in (2, 3):
                wait_tile(sp, 1, t)
            sp.wait_ge(pw_evac, 16)
            sp.dma_start(emb_g[:, :], row(4)).then_inc(emb_g_landed, 16)
            sp.dma_start(keys[:, :, :], keys_t).then_inc(keys_landed, 16)
            slabs_then = (AT_U + 4 * (HOT_FROM + HOT_ITER + 3)) // 2
            with sp.Fori(AT_Q // 2 + 1, slabs_then) as j:
                for s in range(2):
                    load_slab(2 * j + s, s)

            def load_aux(sbn, k):
                sp.dma_start(act_in[k][:, :, :], act_d[bass.ds(sbn, 1)].rearrange("a p b t -> (a p) b t")
                             ).then_inc(aux_landed[k], 16)
                sp.dma_start(gate_in[k][:, :, :].rearrange("p t i -> p (t i)"),
                             pick_d[bass.ds(sbn, 1)].rearrange("a p n -> (a p) n")).then_inc(aux_landed[k], 16)

            for h in range(2):
                sp.wait_ge(pick_stored[h], 16 * (HOT_ITER + 1))
                sp.wait_ge(act_stored[h], 16 * 3)
            load_aux(0, 0)
            with sp.Fori(slabs_then, AT_V // 2 + 1) as j:
                for s in range(2):
                    load_slab(2 * j + s, s)

            def expert_pair(j, last):
                for k in range(2):
                    n = AT_V + 8 * j + 4 * k
                    load_slab(n + 2, 0)
                    load_slab(n + 3, 1)
                    if not (last and k == 1):
                        sp.wait_ge(blk_done, BLK_V)
                        for h in range(2):
                            sp.wait_ge(act_stored[h], 16 * (EB // 2 + 1))
                        sp.wait_ge(ew_made, 2 * j + k + 1)
                        load_aux(2 * j + k + 1, (k + 1) % 2)
                        load_slab(n + 4, 0)
                        load_slab(n + 5, 1)

            with sp.Fori(0, SB // 2 - 1) as j:
                expert_pair(j, False)
            sp.dma_start(ln2_g[:, :], row(5)).then_inc(ln2_landed, 16)
            sp.dma_start(ln2_b[:, :], row(6)).then_inc(ln2_landed, 16)
            expert_pair(SB // 2 - 1, True)
            for t in range(TT):
                wait_tile(sp, 2, t)
                sp.dma_start(out[t * P:(t + 1) * P, :], res[:, t, :]).then_inc(out_stored, 16)
            sp.wait_ge(out_stored, 16 * TT)
            sp.wait_ge(h0_stored, 16 * TT)

        @block.gpsimd
        def _(pool):
            pool.memset(ident[:, :], 0.0)
            pool.iota(iota[:, :], [[1, P]], base=0, channel_multiplier=0,
                      allow_small_or_imprecise_dtypes=True)
            pool.drain()
            pool.affine_select(out=ident[:, :], in_=ident[:, :], compare_op=ALU.not_equal, fill=1.0, base=0,
                               pattern=[[-1, P]], channel_multiplier=1).then_inc(ident_made, 1)
            pool.sem_inc(lo_made, 3)
            for counter, credits in ((evac, 2), (mt_turned, 2), (mt_used, 2), (v_added, 8), (blk_done, 1),
                                     (ef_made, 1), (max_made, 1), (pv_done, 1),
                                     (glu_made, 1), (merged, 1), (ew_made, 1), (v_done, 1), (g_stored[0], 16),
                                     (g_stored[1], 16), (k_stored, 16), (act_stored[0], 16), (act_stored[1], 16),
                                     (pick_stored[0], 16),
                                     (pick_stored[1], 16)):
                pool.sem_inc(counter, credits)
            def scalar_then(out_, a, scalar, b, op0, op1):
                pool.tensor_scalar(prm[:, 19, :], a, scalar, None, op0)
                pool.drain()
                pool.tensor_tensor(out_, prm[:, 19, :], b, op1)

            def series(acc, y, y2, coeffs, last):
                pool.tensor_scalar(acc, y2, coeffs[0], None, ALU.mult)
                for c in coeffs[1:-1]:
                    pool.drain()
                    scalar_then(acc, acc, c, y2, ALU.add, ALU.mult)
                pool.drain()
                scalar_then(acc, acc, coeffs[-1], last, ALU.add, ALU.mult)
                pool.drain()

            names = "lr li dt em x k th y y2 sn c1 ar ai nr den fr fi u v w".split()
            reg = {n: prm[:, j, :] for j, n in enumerate(names)}
            R = lambda n: reg[n]
            pool.wait_ge(prm_landed, 16 * 4)
            pool.tensor_tensor(R("u"), R("lr"), R("lr"), ALU.mult)
            pool.tensor_tensor(R("w"), R("li"), R("li"), ALU.mult)
            pool.drain()
            pool.tensor_tensor(R("den"), R("u"), R("w"), ALU.add).then_inc(den_ready, 1)
            pool.wait_ge(dt_ready, 1)
            pool.tensor_tensor(R("x"), R("lr"), R("dt"), ALU.mult)
            pool.tensor_tensor(R("th"), R("li"), R("dt"), ALU.mult)
            pool.drain()
            pool.tensor_scalar(R("u"), R("x"), -88.0, 88.0, ALU.max, ALU.min)
            pool.drain()
            pool.tensor_scalar(R("y"), R("u"), 1.0 / 64, None, ALU.mult)
            pool.drain()
            series(R("em"), R("y"), R("y"), [1 / fact(n) for n in range(12, 0, -1)], R("y"))
            for _ in range(6):
                scalar_then(R("em"), R("em"), 2.0, R("em"), ALU.add, ALU.mult)
                pool.drain()
            pool.tensor_scalar(R("k"), R("th"), 1 / (2 * np.pi), ROUND, ALU.mult, ALU.add)
            pool.drain()
            pool.tensor_scalar(R("k"), R("k"), -ROUND, None, ALU.add)
            pool.drain()
            for part in (TWO_PI_1, TWO_PI_2, TWO_PI_3):
                scalar_then(R("th"), R("k"), -part, R("th"), ALU.mult, ALU.add)
                pool.drain()
            pool.tensor_scalar(R("th"), R("th"), -PI_F32, PI_F32, ALU.max, ALU.min)
            pool.drain()
            pool.tensor_scalar(R("y"), R("th"), 0.25, None, ALU.mult)
            pool.drain()
            pool.tensor_tensor(R("y2"), R("y"), R("y"), ALU.mult)
            pool.drain()
            series(R("sn"), R("y"), R("y2"), [1 / fact(9), -1 / fact(7), 1 / fact(5), -1 / fact(3), 1.0], R("y"))
            series(R("c1"), R("y"), R("y2"), [-1 / fact(10), 1 / fact(8), -1 / fact(6), 1 / fact(4), -0.5],
                   R("y2"))
            for _ in range(2):
                scalar_then(R("u"), R("c1"), 1.0, R("sn"), ALU.add, ALU.mult)
                pool.drain()
                scalar_then(R("c1"), R("sn"), -2.0, R("sn"), ALU.mult, ALU.mult)
                pool.drain()
                pool.tensor_scalar(R("sn"), R("u"), 2.0, None, ALU.mult)
                pool.drain()
            pool.tensor_scalar(R("u"), R("em"), 1.0, None, ALU.add)
            pool.drain()
            scalar_then(R("ar"), R("c1"), 1.0, R("u"), ALU.add, ALU.mult)
            pool.tensor_tensor(R("ai"), R("sn"), R("u"), ALU.mult)
            pool.tensor_tensor(R("v"), R("em"), R("c1"), ALU.mult)
            pool.tensor_tensor(R("nr"), R("em"), R("c1"), ALU.add)
            pool.drain()
            pool.tensor_tensor(R("nr"), R("nr"), R("v"), ALU.add)
            pool.drain()
            pool.wait_ge(den_ready, 2)
            pool.tensor_tensor(R("u"), R("nr"), R("lr"), ALU.mult)
            pool.tensor_tensor(R("v"), R("ai"), R("li"), ALU.mult)
            pool.drain()
            pool.tensor_tensor(R("fr"), R("u"), R("v"), ALU.add)
            pool.drain()
            pool.tensor_tensor(R("u"), R("ai"), R("lr"), ALU.mult)
            pool.tensor_tensor(R("v"), R("nr"), R("li"), ALU.mult)
            pool.drain()
            pool.tensor_tensor(R("fi"), R("u"), R("v"), ALU.subtract)
            pool.tensor_tensor(R("fr"), R("fr"), R("den"), ALU.mult)
            pool.drain()
            pool.tensor_tensor(R("fi"), R("fi"), R("den"), ALU.mult)
            pool.drain()
            f_wide = [R(n).unsqueeze(2).to_broadcast([P, QN, GCH]) for n in ("fr", "fi")]
            half_t1 = t1[:, 0:QN * GCH].rearrange("p (q c) -> p q c", c=GCH)
            half_t2 = t2[:, 0:QN * GCH].rearrange("p (q c) -> p q c", c=GCH)
            pool.wait_ge(b_landed, 32)
            cmul(pool, bb[:, 0], bb[:, 1], f_wide, [b_raw[:, 0], b_raw[:, 1]], half_t1, half_t2)
            def low_part(j, slot):
                for half in range(2):
                    part = slice(half * HALF, (half + 1) * HALF)
                    pool.wait_ge(hi_made, 4 * j + 2 * slot + half + 1)
                    pool.tensor_tensor(wlo[slot][:, part], raw[slot][:, part],
                                       whi[slot][:, part].bitcast(F32), ALU.subtract).then_inc(lo_made, 1)

            low_part(0, 0)
            pool.memset(pow_up[:, 0, :, 0:1], 1.0)
            pool.memset(pow_up[:, 1, :, 0:1], 0.0)
            pool.tensor_copy(pow_up[:, 0, :, 1], R("ar"))
            pool.tensor_copy(pow_up[:, 1, :, 1], R("ai"))
            pool.drain()
            for lo, n in ((1, 1), (2, 2), (4, 4)):
                by = [pow_up[:, ri, :, lo:lo + 1].to_broadcast([P, QN, n]) for ri in range(2)]
                ta, tb = (z[:, 0:QN * n].rearrange("p (q n) -> p q n", n=n) for z in (t1, t2))
                cmul(pool, pow_up[:, 0, :, lo + 1:lo + n + 1], pow_up[:, 1, :, lo + 1:lo + n + 1],
                     [pow_up[:, ri, :, 1:n + 1] for ri in range(2)], by, ta, tb)
            pool.sem_inc(prm_ready, 1)

            def low_parts(first, end):
                with pool.Fori(first, end) as j:
                    for slot in range(2):
                        low_part(j, slot)

            def biases(b, first):
                for n, t in enumerate(POOL_TILES[first]):
                    pool.wait_ge(gained, pool_count(first) + n + 1)
                    pool.tensor_tensor(res[:, t, :], res[:, t, :], b[:, :], ALU.add).then_inc(pool_h_ready, 1)

            low_part(0, 1)
            low_parts(1, AT_Q // 2)
            biases(ln_b, 1)
            low_parts(AT_Q // 2, N_SLABS // 2)
            biases(ln2_b, 2)

        @block.scalar
        def _(act):
            copy = ACT.Copy

            def normalise(tiles, first, t):
                act.wait_ge(rstd_ready, TT * first + t + 1)
                act.activation(tiles[:, t, :], tiles[:, t, :], ACT.Identity, bias=shift[:, t:t + 1],
                               scale=rstd[:, t:t + 1]).then_inc(xn_ready, 1)

            def std_of(first, t):
                act.wait_ge(var_ready, TT * first + t + 1)
                act.activation(std[:, t:t + 1], std[:, t:t + 1], ACT.Sqrt).then_inc(std_ready, 1)

            def all_stds(first):
                act.wait_ge(var_ready, TT * (first + 1))
                act.activation(std[:, :], std[:, :], ACT.Sqrt).then_inc(std_ready, TT)

            def turned_hi(dst, first):
                for t in range(TT):
                    for g in range(4):
                        act.wait_ge(turned, 16 * first + 4 * t + g + 1)
                        act.activation(dst[:, 4 * g:4 * g + 4, t * P:(t + 1) * P],
                                       ps[4 * (t % 2) + g][:, :].rearrange("p (c t) -> p c t", c=4),
                                       copy).then_inc(turn_hi, 1)

            act.wait_ge(k_zeroed, 1)
            for q in (0, CB_Q):
                act.dma_start(k_d[:, q:q + CB_Q, 0:(LC - 1) * GCH], k_tab[0:GCH, :, 0:(LC - 1) * GCH]
                              ).then_inc(k_zeroed, 16)
            act.wait_ge(prm_landed, 16 * 4)
            act.activation(prm[:, 2, :], prm[:, 2, :], ACT.Exp).then_inc(dt_ready, 1)
            for t in range(TT):
                std_of(0, t)
                normalise(xt, 0, t)
            act.wait_ge(raw_landed[0], 16)
            for half in range(2):
                part = slice(half * HALF, (half + 1) * HALF)
                act.activation(whi[0][:, part], raw[0][:, part], copy).then_inc(hi_made, 1)
            turned_hi(h0_hi, 0)
            for t in range(TT):
                act.wait_ge(h_ready, t + 1)
                act.dma_start(h0_d[t], xt[:, t, :]).then_inc(h0_stored, 16)

            with act.Fori(0, HEADS) as i:
                def split_next(b):
                    nxt = b + 1
                    slot = nxt % 2
                    act.wait_ge(raw_landed[slot], 16 * (4 * i + nxt // 2 + 1))
                    act.wait_ge(blk_done, 8 * i + b + 1)
                    for half in range(2):
                        cols = slice(half * HALF, (half + 1) * HALF)
                        act.activation(whi[slot][:, cols], raw[slot][:, cols], copy).then_inc(hi_made, 1)

                def wait_block(b):
                    act.wait_ge(blk_done, 8 * i + b + 2)

                def step(b):
                    split_next(b)
                    wait_block(b)

                def store_gate(j):
                    act.wait_ge(g_stored[j % 2], 16 * (2 * i + j // 2 + 1))
                    act.activation(g_out[j % 2][:, :], ps_p[j % 2][:, :], copy)
                    act.drain()
                    act.dma_start(gate_d[bass.ds(4 * i + j, 1)].rearrange("a p n -> (a p) n"),
                                  g_out[j % 2][:, :]).then_inc(g_stored[j % 2], 16)

                def exps(t):
                    n = (t + 1) * P
                    act.wait_ge(max_made, TT * i + t + 2)
                    act.activation(prob[:, t, 0:n], prob[:, t, 0:n], ACT.Exp, bias=neg_max[:, t:t + 1],
                                   accum_out=row_sum[:, t:t + 1]).then_inc(exp_made, 1)

                def s5_out():
                    act.wait_ge(y_done, i + 1)
                    act.activation(y_sc[:, :, :], ps_x[:, :].rearrange("p (g n) -> p g n", n=NC), copy)
                    act.drain()
                    act.dma_start(y_d, y_sc[:, :, :]).then_inc(y_stored, 16)

                step(0)
                act.wait_ge(prm_ready, 1)
                act.activation(u_cs[:, :, :], ps_p[0][:, :].rearrange("p (c s) -> p s c", s=LC), copy)
                act.drain()
                act.dma_start(u_d, u_cs[:, :, :]).then_inc(u_stored, 16)

                step(1)
                act.activation(q_h[:, :], ps_p[1][:, :], copy).then_inc(qkv_made, 1)
                act.wait_ge(e_turned, i + 1)
                for ri in range(2):
                    last = act.activation(in_map[:, ri, :, :], ps_t[ri][:, :].rearrange("p (q n) -> p q n", q=CB_Q),
                                          copy)
                last.then_inc(in_map_made, 1)

                step(2)
                act.activation(k_h[:, :], ps_p[0][:, :], copy).then_inc(qkv_made, 1)
                act.wait_ge(k_made, i + 1)
                for r in range(2):
                    act.dma_start(k_d[:, r::2, (LC - 1) * GCH:], k_tab[GCH * r:GCH * (r + 1), :, :]
                                  ).then_inc(k_stored, 16)
                act.wait_ge(bu_done, i + 1)
                act.activation(h_st[:, :, :, 1:], ps_s[0][:, :].rearrange("p (r q n) -> p r q n", r=2, q=CB_Q),
                               copy).then_inc(h_filled, 1)

                step(3)
                act.activation(v_h[:, :], ps_p[1][:, :], copy).then_inc(qkv_made, 1)

                step(4)
                store_gate(0)

                split_next(5)
                exps(0)
                exps(1)
                wait_block(5)
                store_gate(1)
                act.wait_ge(v_turned, i + 1)
                act.activation(v_keys[:, :, :], ps_t[0][:, :].rearrange("p (k n) -> p k n", k=TT),
                               copy).then_inc(v_made, 1)

                split_next(6)
                exps(2)
                exps(3)
                s5_out()
                wait_block(6)
                store_gate(2)
                for t in range(TT):
                    act.wait_ge(pt_done, TT * i + t + 1)
                    act.activation(prob_t[:, 0:t + 1, t * P:(t + 1) * P],
                                   ps_pt[t][:, 0:(t + 1) * P].rearrange("p (k n) -> p k n", n=P),
                                   copy).then_inc(pt_made, 1)

                step(7)
                store_gate(3)
                act.wait_ge(y_landed, 128 * (i + 1))
                act.activation(y_ssm[:, bass.ds(i, 1), :].rearrange("p o (c s) -> p (o s) c", s=LC),
                               y_cs[:, :, :], ACT.Gelu_apprx_tanh).then_inc(branch_made, 1)
                act.wait_ge(pv_done, i + 2)
                act.activation(y_attn[:, bass.ds(i, 1), :], ps_y[:, :].unsqueeze(1), copy).then_inc(branch_made, 1)
            act.wait_ge(g_stored[0], 16 * (2 * HEADS + 1))
            act.wait_ge(g_stored[1], 16 * (2 * HEADS + 1))
            act.wait_ge(branch_made, 2 * HEADS)
            for hi, y in ((ys_hi, y_ssm), (ya_hi, y_attn)):
                for c in range(0, WC, 2):
                    act.activation(hi[:, c:c + 2, :], y[:, c:c + 2, :], copy).then_inc(split_hi_made, 1)

            def next_hi(at, j, s, used_sem, used):
                slot = (s + 1) % 2
                act.wait_ge(raw_landed[slot], 16 * (at // 2 + j + 1 + s))
                act.wait_ge(used_sem, used)
                for half in range(2):
                    part = slice(half * HALF, (half + 1) * HALF)
                    act.activation(whi[slot][:, part], raw[slot][:, part], copy).then_inc(hi_made, 1)

            with act.Fori(0, N_GLU // 2) as j:
                for s in range(2):
                    m = 4 * j + 2 * s
                    next_hi(AT_GLU, j, s, blk_done, BLK_GLU + m)
                    act.wait_ge(glu_made, m + 1)
                    for half in range(2):
                        act.wait_ge(blk_done, BLK_GLU + m + half + 1)
                        act.activation(glu_s[half][:, :], ps_p[half][:, :], ACT.Sigmoid).then_inc(evac, 1)

            def load_gates(d, k):
                for h in range(2):
                    act.dma_start(gates[k][:, h, :], gate_d[bass.ds(d + DC * h, 1)].rearrange("a p n -> (a p) n")
                                  ).then_inc(gates_landed[k], 16)

            act.wait_ge(split_lo_made, WC)
            load_gates(0, 0)

            def up_pair(j, last):
                for s in range(2):
                    d = 2 * j + s
                    next_hi(AT_UP, j, s, blk_done, BLK_UP + 2 * d)
                    act.wait_ge(merged, d + 1)
                    if not (last and s == 1):
                        load_gates(d + 1, (s + 1) % 2)
                    act.wait_ge(gates_landed[s], 32 * (j + 1))
                    act.activation(gates[s][:, :, :], gates[s][:, :, :], ACT.Sigmoid).then_inc(sig_made, 1)

            with act.Fori(0, DC // 2 - 1) as j:
                up_pair(j, False)
            up_pair(DC // 2 - 1, True)

            act.wait_ge(blk_done, BLK_OUT)
            act.wait_ge(h0_stored, 16 * TT)
            for t in range(TT):
                act.dma_start(res[:, t, :], h0_d[t]).then_inc(res_landed, 16)

            def projections(at, blk0, o0, func, start=0, end=DC // 2, more=None):
                with act.Fori(start, end) as j:
                    for s in range(2):
                        o = 2 * j + s
                        next_hi(at, j, s, blk_done, blk0 + o)
                        act.wait_ge(blk_done, blk0 + o + 1)
                        act.wait_ge(mt_turned, o0 + o + 1)
                        act.activation(mt[s][:, :], ps_p[s][:, :], func).then_inc(evac, 1)
                        if more is not None:
                            more(o)

            projections(AT_OUT, BLK_OUT, 0, copy)

            def embedding_out(q):
                t, c = q // 4, q % 4
                act.wait_ge(pw_done, q + 1)
                act.activation(emb[:, t, c * 512:(c + 1) * 512], ps[2 + q % 2][:, :], copy).then_inc(pw_evac, 1)

            for q in (0, 1):
                embedding_out(q)
            all_stds(1)
            for t in range(TT):
                embedding_out(2 * t + 2)
                normalise(res, 1, t)
                embedding_out(2 * t + 3)
            for q in range(10, 16):
                embedding_out(q)
            turned_hi(h1_hi, 1)

            def squares(o):
                act.drain()
                act.activation(junk[:, :], emb[:, :, :].rearrange("p t d -> p (t d)")[:, bass.ds(o * 1024, 1024)],
                               ACT.Square, accum_out=sq_sum[:, bass.ds(o, 1)]).then_inc(sq_made, 1)

            projections(AT_Q, BLK_Q, N_OUT, copy, 0, DC // 4, squares)
            projections(AT_Q, BLK_Q, N_OUT, copy, DC // 4, DC // 2)
            act.wait_ge(ms_ready, 1)
            act.activation(sq_tot[:, :], sq_tot[:, :], ACT.Sqrt).then_inc(rms_ready, 1)
            projections(AT_GATE, BLK_GATE, N_OUT + N_Q, ACT.Sigmoid)

            def experts(j, hots):
                for s in range(4):
                    e = 4 * j + s
                    slot = (s + 1) % 2
                    act.wait_ge(raw_landed[slot], 16 * (AT_U // 2 + 2 * j + (s + 1) // 2 + 1))
                    act.wait_ge(blk_done, BLK_U + e)
                    for half in range(2):
                        part = slice(half * HALF, (half + 1) * HALF)
                        act.activation(whi[slot][:, part], raw[slot][:, part], copy).then_inc(hi_made, 1)
                    act.wait_ge(blk_done, BLK_U + e + 1)
                    if not hots:
                        act.wait_ge(mt_turned, N_OUT + N_Q + N_GATE + 2)
                    act.wait_ge(act_stored[s % 2], 16 * (2 * j + s // 2 + 1))
                    act.activation(mt[s % 2][:, :], ps_p[s % 2][:, :], ACT.Gelu_apprx_tanh).then_inc(evac, 1)
                    act.drain()
                    act.dma_start(act_d[bass.ds(j, 1), :, s, :].rearrange("a p t -> (a p) t"),
                                  mt[s % 2][:, :]).then_inc(act_stored[s % 2], 16)
                    if hots:
                        it, h = j - HOT_FROM, s // 2
                        if s % 2 == 0:
                            act.wait_ge(pick_stored[h], 16 * (it + 1))
                        act.wait_ge(hot_done, 4 * it + s + 1)
                        for m in range(HOT // 2):
                            last = act.activation(hot_out(s, m), hot_in(m)[:, 0], copy)
                        last.then_inc(hot_moved, 1)
                    if hots and s % 2 == 1:
                        act.wait_ge(hot_evac, 2 * it + h + 1)
                        act.dma_start(pick_d[:, :, bass.ds(64 * (2 * it + h), 64)].rearrange("b p n -> p b n"),
                                      gate_st[h][:, :, :, :].rearrange("p b t i -> p b (t i)")
                                      ).then_inc(pick_stored[h], 16)

            with act.Fori(0, HOT_FROM - 1) as j:
                experts(j, False)
            act.wait_ge(picks_made, 1)
            act.activation(sel_g[:, :, :], sel_g[:, :, :], ACT.Exp).then_inc(exps_made, 1)
            with act.Fori(HOT_FROM - 1, HOT_FROM) as j:
                experts(j, False)
            act.wait_ge(picks_turned, 1)
            act.activation(pick_i[:, :], ps_s[0][:, :], copy)
            act.activation(pick_j[:, :], ps_s[1][:, :], copy)
            act.activation(pick_gh[:, :], ps_t[0][:, :], copy).then_inc(pick_gh_made, 1)
            with act.Fori(HOT_FROM, HOT_FROM + HOT_ITER) as j:
                experts(j, True)
            with act.Fori(HOT_FROM + HOT_ITER, SB) as j:
                experts(j, False)

            def expert_pair(j, last):
                for q in range(8):
                    if last and q == 7:
                        continue
                    slot = (q + 1) % 2
                    act.wait_ge(raw_landed[slot], 16 * (AT_V // 2 + 4 * j + (q + 1) // 2 + 1))
                    act.wait_ge(v_done, 4 * (8 * j + q) + 1)
                    for half in range(2):
                        part = slice(half * HALF, (half + 1) * HALF)
                        act.activation(whi[slot][:, part], raw[slot][:, part], copy).then_inc(hi_made, 1)

            with act.Fori(0, SB // 2 - 1) as j:
                expert_pair(j, False)
            expert_pair(SB // 2 - 1, True)
            for t in range(TT):
                std_of(2, t)
                normalise(res, 2, t)

        @block.tensor
        def _(pe):
            def block_of(bank, slot, n, rhs_hi, rhs_lo, chunk_ready=None):
                for half in range(2):
                    pe.wait_ge(lo_made, 2 * n + half + 4)
                    for c in range(8 * half, 8 * half + 8):
                        cols = slice(c * P, (c + 1) * P)
                        if chunk_ready is not None:
                            chunk_ready(c)
                        pe.matmul(bank[:, :], whi[slot][:, cols], rhs_hi[:, c, :], start=c == 0, stop=False)
                        pe.matmul(bank[:, :], whi[slot][:, cols], rhs_lo[:, c, :], start=False, stop=False)
                        last = pe.matmul(bank[:, :], wlo[slot][:, cols], rhs_hi[:, c, :], start=False,
                                         stop=c == DC - 1)
                last.then_inc(blk_done, 1)

            def turn(tiles, first):
                if not first:
                    pe.wait_ge(ident_made, 1)
                for t in range(TT):
                    wait_tile(pe, first, t)
                    for g in range(4):
                        if t >= 2:
                            pe.wait_ge(turn_lo, 16 * first + 4 * (t - 2) + g + 1)
                        for c in range(4):
                            last = pe.transpose(ps[4 * (t % 2) + g][:, c * P:(c + 1) * P],
                                                tiles[:, t, (4 * g + c) * P:(4 * g + c + 1) * P], ident[:, :])
                        last.then_inc(turned, 1)

            def turned_ready(first):
                def ready(c):
                    if c % 4 == 0:
                        pe.wait_ge(turn_lo, 16 * first + 12 + c // 4 + 1)
                return ready

            def merged_ready(c):
                if c == 0:
                    pe.wait_ge(merged, DC - 2 + 1)
                elif c >= DC - 2:
                    pe.wait_ge(merged, c + 2)

            turn(xt, 0)
            with pe.Fori(0, HEADS) as i:
                def blk(b):
                    block_of(ps_p[b % 2], b % 2, 8 * i + b, h0_hi, h0_lo, turned_ready(0) if b == 0 else None)

                def scores(t):
                    if t >= 2:
                        pe.wait_ge(max_made, TT * i + t)
                    pe.matmul(ps_s[t % 2][:, 0:(t + 1) * P], q_h[:, t * P:(t + 1) * P], k_h[:, 0:(t + 1) * P],
                              start=True, stop=True).then_inc(sc_done, 1)

                blk(0)
                blk(1)
                pe.wait_ge(ef_made, i + 2)
                for ri in range(2):
                    for q in range(CB_Q):
                        last = pe.transpose(ps_t[ri][:, q * P:(q + 1) * P],
                                            e_tab[:, ri, q, :, :].rearrange("p s c -> p (s c)"), ident[:, :])
                last.then_inc(e_turned, 1)
                for q in range(CB_Q):
                    for ri in range(2):
                        last = pe.matmul(ps_x[0:2 * GCH, q * P:(q + 1) * P],
                                         bb_pair[:, ri, q, :, :].rearrange("p r c -> p (r c)"),
                                         f_tab[:, ri, q, 0:LC, :].rearrange("p s c -> p (s c)"),
                                         start=ri == 0, stop=ri == 1)
                last.then_inc(k_done, 1)
                blk(2)
                pe.wait_ge(in_map_made, i + 1)
                pe.wait_ge(u_landed, 128 * (i + 1))
                for r in range(2):
                    for ri in range(2):
                        for q in range(CB_Q):
                            col = (ri * CB_Q + q) * NC
                            last = pe.matmul(ps_s[0][ST * r:ST * (r + 1), col:col + NC],
                                             in_map[:, ri, q, ST * r:ST * (r + 1)], u_sc[:, 2 * q + r, :],
                                             start=True, stop=True)
                last.then_inc(bu_done, 1)
                blk(3)
                pe.wait_ge(qkv_made, 3 * i + 2)
                pe.wait_ge(h_filled, i + 1)
                scores(0)
                scores(1)
                blk(4)
                pe.wait_ge(qkv_made, 3 * i + 3)
                for t in range(TT):
                    last = pe.transpose(ps_t[0][:, t * P:(t + 1) * P], v_h[:, t * P:(t + 1) * P], ident[:, :])
                last.then_inc(v_turned, 1)
                blk(5)
                scores(2)
                scores(3)
                pe.wait_ge(toep_landed, 128 * (i + 1))
                pe.wait_ge(scanned, i + 1)
                for q in range(CB_Q):
                    for ri in range(2):
                        pe.matmul(ps_x[:, 2 * q * NC:2 * (q + 1) * NC],
                                  f_tab[:, ri, q, 1:, :].rearrange("p s c -> p (s c)"),
                                  h_pair[:, ri, q, :, :].rearrange("p r n -> p (r n)"), start=ri == 0, stop=False)
                    for r in range(2):
                        g = 2 * q + r
                        last = pe.matmul(ps_x[:, g * NC:(g + 1) * NC], toep[:, g, :], u_sc[:, g, :], start=False,
                                         stop=r == 1)
                last.then_inc(y_done, 1)
                blk(6)
                pe.wait_ge(v_made, i + 1)
                for t in range(TT):
                    pe.wait_ge(prob_made, TT * i + t + 1)
                    for k in range(t + 1):
                        last = pe.transpose(ps_pt[t][:, k * P:(k + 1) * P], prob[:, t, k * P:(k + 1) * P],
                                            ident[:, :])
                    last.then_inc(pt_done, 1)
                blk(7)
                pe.wait_ge(pt_made, TT * (i + 1))
                for k in range(TT):
                    last = pe.matmul(ps_y[:, k * P:], v_keys[:, k, :], prob_t[:, k, k * P:], start=k == 0,
                                     stop=k == TT - 1)
                last.then_inc(pv_done, 1)

            def two_blocks(n, slot, blk, rhs, pieces=False):
                for half in range(2):
                    pe.wait_ge(lo_made, 2 * n + half + 4)
                    pe.wait_ge(evac, blk - BLK_GLU + half + 1)
                    if not pieces and half == 1:
                        pe.wait_ge(glu_made, WC + 1)
                    hi, lo = rhs[half]
                    for c in range(WC):
                        if pieces and c % 2 == 0:
                            pe.wait_ge(split_lo_made, c // 2 + 1)
                        part = slice(half * HALF + c * P, half * HALF + (c + 1) * P)
                        pe.matmul(ps_p[half][:, :], whi[slot][:, part], hi[:, c, :], start=c == 0, stop=False)
                        pe.matmul(ps_p[half][:, :], whi[slot][:, part], lo[:, c, :], start=False, stop=False)
                        last = pe.matmul(ps_p[half][:, :], wlo[slot][:, part], hi[:, c, :], start=False,
                                         stop=c == WC - 1)
                    last.then_inc(blk_done, 1)

            with pe.Fori(0, N_GLU // 2) as j:
                for s in range(2):
                    two_blocks(AT_GLU + 2 * j + s, s, BLK_GLU + 4 * j + 2 * s, [(ys_hi, ys_lo)] * 2, True)
            pe.wait_ge(split_lo_made, WC)
            with pe.Fori(0, DC // 2) as j:
                for s in range(2):
                    two_blocks(AT_UP + 2 * j + s, s, BLK_UP + 4 * j + 2 * s, [(ya_hi, ya_lo), (y2_hi, y2_lo)])
            def projections(at, blk0, o0, rhs_hi, rhs_lo, second, chunk_ready=None):
                def first(o, s, ready=None):
                    pe.wait_ge(evac, blk0 + o - BLK_GLU + 1)
                    block_of(ps_p[s], s, at + o, rhs_hi, rhs_lo, ready)

                def then(o, s):
                    pe.wait_ge(evac, blk0 + o - BLK_GLU + 3)
                    pe.wait_ge(mt_used, o0 + o + 1)
                    second(o, s).then_inc(mt_turned, 1)

                first(0, 0, chunk_ready)
                with pe.Fori(0, DC // 2 - 1) as j:
                    first(2 * j + 1, 1)
                    then(2 * j, 0)
                    first(2 * j + 2, 0)
                    then(2 * j + 1, 1)
                first(DC - 1, 1)
                then(DC - 2, 0)
                then(DC - 1, 1)

            def turn_block(o, s):
                for t in range(TT):
                    last = pe.transpose(ps_t[s][:, t * P:(t + 1) * P], mt[s][:, t * P:(t + 1) * P], ident[:, :])
                return last

            def key_scores(o, s):
                pe.wait_ge(keys_landed, 16)
                for t in range(TT):
                    last = pe.matmul(ps_t[s][:, t * P:(t + 1) * P], mt[s][:, t * P:(t + 1) * P],
                                     keys[:, bass.ds(o, 1), :].rearrange("p a n -> p (a n)"), start=True, stop=True)
                return last

            projections(AT_OUT, BLK_OUT, 0, m_hi, m_lo, turn_block, merged_ready)
            pe.wait_ge(ple_landed, 32)
            for q in range(16):
                t, c = q // 4, q % 4
                if q >= 2:
                    pe.wait_ge(pw_evac, q - 1)
                for k in range(2):
                    last = pe.matmul(ps[2 + q % 2][:, :], p_sb[:, k, t * P:(t + 1) * P],
                                     pw_sb[:, k, c * 512:(c + 1) * 512], start=k == 0, stop=k == 1)
                last.then_inc(pw_done, 1)
            pe.wait_ge(pw_evac, 16)
            turn(res, 1)
            projections(AT_Q, BLK_Q, N_OUT, h1_hi, h1_lo, key_scores, turned_ready(1))
            projections(AT_GATE, BLK_GATE, N_OUT + N_Q, h1_hi, h1_lo, turn_block)
            def experts(j, hots):
                for s in range(4):
                    e = 4 * j + s
                    pe.wait_ge(evac, BLK_U + e - BLK_GLU + 1)
                    block_of(ps_p[s % 2], s % 2, AT_U + e, h1_hi, h1_lo)
                    if hots:
                        pe.wait_ge(hot_made, e - 4 * HOT_FROM + 1)
                        for k in range(HOT):
                            last = pe.matmul(ps[2 + k // 2][:, (k % 2) * 2 * P:(k % 2 + 1) * 2 * P],
                                             hot_j[:, k, :], hot_g[:, k, :, :].rearrange("p z i -> p (z i)"),
                                             start=True, stop=True)
                        last.then_inc(hot_done, 1)

            with pe.Fori(0, HOT_FROM) as j:
                experts(j, False)
            pe.wait_ge(gates_made, 1)
            for bank, sel in ((ps_s[0], sel_i), (ps_s[1], sel_j), (ps_t[0], sel_g)):
                for t in range(TT):
                    last = pe.transpose(bank[:, t * P:(t + 1) * P], sel[:, t, :], ident[:, :])
            last.then_inc(picks_turned, 1)
            with pe.Fori(HOT_FROM, HOT_FROM + HOT_ITER) as j:
                experts(j, True)
            with pe.Fori(HOT_FROM + HOT_ITER, SB) as j:
                experts(j, False)

            with pe.Fori(0, SB // 2) as j:
                for k in range(2):
                    pe.wait_ge(ew_made, 2 * j + k + 2)
                    for c in range(4):
                        q = 4 * k + c
                        n = AT_V + 8 * j + q
                        slot = q % 2
                        if c == 1:
                            pe.wait_ge(evac, BLK_V - BLK_GLU + 2)
                        for t in range(TT):
                            bank = ps[4 * ((c + 1) % 2) + t]
                            pe.wait_ge(v_added, 4 * (8 * j + q) + t + 1)
                            for b in range(4):
                                if t == 0 and b % 2 == 0:
                                    pe.wait_ge(lo_made, 2 * n + b // 2 + 4)
                                rows = slice(t * P, (t + 1) * P)
                                part = slice(b * 512, (b + 1) * 512)
                                pe.matmul(bank[:, :], ew_hi[k][:, b, rows], whi[slot][:, part], start=b == 0,
                                          stop=False)
                                pe.matmul(bank[:, :], ew_hi[k][:, b, rows], wlo[slot][:, part], start=False,
                                          stop=False)
                                last = pe.matmul(bank[:, :], ew_lo[k][:, b, rows], whi[slot][:, part],
                                                 start=False, stop=b == 3)
                            last.then_inc(v_done, 1)

        @block.vector
        def _(dve):
            def tt(o, a, b, op):
                return dve.tensor_tensor(o, a, b, op)

            def quarter(tiles, t, c):
                dve.bn_stats(stat[:, t, c, :], tiles[:, t, c * 512:(c + 1) * 512])

            def variance(t):
                dve.bn_aggr(mv[:, t, :], stat[:, t, :, :].rearrange("p a b -> p (a b)"))
                dve.drain()
                dve.tensor_scalar(std[:, t:t + 1], mv[:, t, 1:2], EPS, None, ALU.add).then_inc(var_ready, 1)

            def scale(first, t):
                dve.wait_ge(std_ready, TT * first + t + 1)
                dve.reciprocal(rstd[:, t:t + 1], std[:, t:t + 1])
                dve.drain()
                dve.scalar_tensor_tensor(shift[:, t:t + 1], mv[:, t, 0:1], -1.0, rstd[:, t:t + 1], ALU.mult,
                                         ALU.mult).then_inc(rstd_ready, 1)

            def gain(tiles, g, first, t):
                dve.wait_ge(xn_ready, TT * first + t + 1)
                last = tt(tiles[:, t, :], tiles[:, t, :], g[:, :], ALU.mult)
                if t in POOL_TILES[first]:
                    last.then_inc(gained, 1)

            def bias(tiles, b, t):
                dve.drain()
                tt(tiles[:, t, :], tiles[:, t, :], b[:, :], ALU.add).then_inc(h_ready, 1)

            def normalised(tiles, g, b, first):
                for t in range(TT):
                    variance(t)
                for t in range(TT):
                    scale(first, t)
                for t in range(TT):
                    gain(tiles, g, first, t)
                    if t not in POOL_TILES[first]:
                        bias(tiles, b, t)

            def turned_lo(dst_lo, dst_hi, first):
                for t in range(TT):
                    for g in range(4):
                        dve.wait_ge(turn_hi, 16 * first + 4 * t + g + 1)
                        tt(dst_lo[:, 4 * g:4 * g + 4, t * P:(t + 1) * P],
                           ps[4 * (t % 2) + g][:, :].rearrange("p (c t) -> p c t", c=4),
                           dst_hi[:, 4 * g:4 * g + 4, t * P:(t + 1) * P].bitcast(F32),
                           ALU.subtract).then_inc(turn_lo, 1)

            dve.memset(k_tab[:, :, :], 0.0).then_inc(k_zeroed, 1)
            dve.wait_ge(den_ready, 1)
            dve.reciprocal(prm[:, 14, :], prm[:, 14, :]).then_inc(den_ready, 1)
            for t in range(TT):
                dve.wait_ge(x_landed[t], 16)
                for c in range(4):
                    quarter(xt, t, c)
                dve.drain()
                variance(t)
                scale(0, t)
                if t > 0:
                    if t == 1:
                        dve.wait_ge(ln_in_landed, 32)
                    gain(xt, g_in, 0, t - 1)
                    bias(xt, b_ln_in, t - 1)
            gain(xt, g_in, 0, 3)
            bias(xt, b_ln_in, 3)
            turned_lo(h0_lo, h0_hi, 0)

            dve.memset(h_st[:, :, :, 0:1], 0.0)
            dve.memset(bb_pair[:, :, :, :, :], 0.0)
            dve.memset(band[0:64, 192:256], -1e30)
            dve.wait_ge(prm_ready, 1)
            for m in range(LC + 1):
                dve.tensor_copy(pow_dn[:, :, :, LC - m:LC - m + 1], pow_up[:, :, :, m:m + 1])
            dve.tensor_copy(lev[:, :, :, 0:1], pow_up[:, :, :, LC:LC + 1])
            dve.drain()
            for k in range(5):
                a = [lev[:, ri, :, k] for ri in range(2)]
                cmul(dve, lev[:, 0, :, k + 1], lev[:, 1, :, k + 1], a, a, t1[:, 0:QN], t2[:, 0:QN])

            with dve.Fori(0, HEADS) as i:
                dve.wait_ge(pv_done, i + 1)
                sl = bass.ds(CB_Q * i, CB_Q)
                dve.tensor_copy(pow_up_s[:, :, :, :], pow_up[:, :, sl, :])
                dve.tensor_copy(pow_dn_s[:, :, :, :], pow_dn[:, :, sl, :])
                dve.tensor_copy(lev_s[:, :, :, :], lev[:, :, sl, :])
                dve.tensor_copy(bb_s[:, :, :, :], bb[:, :, sl, :])
                for r in range(2):
                    rows = slice(ST * r, ST * (r + 1))
                    dve.tensor_copy(bb_pair[rows, :, :, r, :], bb[rows, :, sl, :])
                tt(d_diag[:, :, :, :].rearrange("p q r c -> p q (r c)"),
                   d_bc[:, bass.ds(i * P, P)].rearrange("p (q c) -> p q c", q=CB_Q),
                   ident[0:2 * GCH, 0:2 * GCH].unsqueeze(1).to_broadcast([2 * GCH, CB_Q, 2 * GCH]), ALU.mult)
                dve.drain()
                ta, tb = (z[:, 0:512].rearrange("p (q s c) -> p q s c", q=CB_Q, s=LC) for z in (t1, t2))
                wide = [P, CB_Q, LC, GCH]
                cmul(dve, e_tab[:, 0], e_tab[:, 1],
                     [pow_dn_s[:, ri, :, 1:].unsqueeze(3).to_broadcast(wide) for ri in range(2)],
                     [bb_s[:, ri].unsqueeze(2).to_broadcast(wide) for ri in range(2)], ta, tb)
                dve.wait_ge(c_landed, 16 * (i + 1))
                ta, tb = (z[:, 0:576].rearrange("p (q s c) -> p q s c", q=CB_Q, s=LC + 1) for z in (t1, t2))
                wide = [P, CB_Q, LC + 1, GCH]
                cmul(dve, f_tab[:, 0], f_tab[:, 1],
                     [pow_up_s[:, ri].unsqueeze(3).to_broadcast(wide) for ri in range(2)],
                     [c_s[:, ri].unsqueeze(2).to_broadcast(wide) for ri in range(2)], ta, tb,
                     minus_im=True).then_inc(ef_made, 1)
                dve.wait_ge(k_done, i + 1)
                dve.wait_ge(k_stored, 32 * i + 16)
                dve.wait_ge(k_zeroed, 33)
                dve.tensor_copy(k_tab[:, :, :], ps_x[0:2 * GCH, :].rearrange("p (q n) -> p q n", q=CB_Q))
                for r in range(2):
                    dve.drain()
                    last = tt(k_tab[:, :, 0:GCH], k_tab[:, :, 0:GCH], d_diag[:, :, r, :], ALU.add)
                last.then_inc(k_made, 1)
                dve.wait_ge(h_filled, i + 1)
                for k in range(6):
                    n = NC - 2**k
                    src = h_st[:, :, :, 1:1 + n]
                    ta, tb = (z[:, 0:512].rearrange("p (r q n) -> p r q n", r=2, q=CB_Q)[:, :, :, 0:n]
                              for z in (t1, t2))
                    a_re, a_im = (lev_s[:, ri, :, k:k + 1].unsqueeze(1).to_broadcast([P, 2, CB_Q, n])
                                  for ri in range(2))
                    tt(ta, src, a_re, ALU.mult)
                    tt(tb, src, a_im, ALU.mult)
                    dve.drain()
                    tt(ta[:, 0], ta[:, 0], tb[:, 1], ALU.subtract)
                    tt(ta[:, 1], ta[:, 1], tb[:, 0], ALU.add)
                    dve.drain()
                    tt(h_st[:, :, :, 1 + 2**k:], h_st[:, :, :, 1 + 2**k:], ta, ALU.add)
                    dve.drain()
                for r in range(2):
                    rows = slice(ST * r, ST * (r + 1))
                    dve.memset(h_pair[rows, :, :, 1 - r, :], 0.0)
                    last = dve.tensor_copy(h_pair[rows, :, :, r, :], h_st[rows, :, :, 0:NC])
                last.then_inc(scanned, 1)
                dve.drain()
                dve.wait_ge(band_landed, 32 * (i + 1))

                def bias_and_max(t):
                    n, near = (t + 1) * P, min((t + 1) * P, 2 * P)
                    dve.wait_ge(sc_done, TT * i + t + 1)
                    bank = ps_s[t % 2]
                    dve.scalar_tensor_tensor(prob[:, t, n - near:n], bank[:, n - near:n], SCALE,
                                             band[:, 2 * P - near:], ALU.mult, ALU.add)
                    if n > near:
                        dve.tensor_scalar(prob[:, t, 0:n - near], bank[:, 0:n - near], SCALE, band[:, 0:1],
                                          ALU.mult, ALU.add)
                    dve.drain()
                    dve.tensor_reduce(row_max[:, t:t + 1], prob[:, t, 0:n], AX.X, ALU.max)
                    dve.drain()
                    dve.tensor_scalar(neg_max[:, t:t + 1], row_max[:, t:t + 1], -1.0, None,
                                      ALU.mult).then_inc(max_made, 1)

                def divide(t):
                    n = (t + 1) * P
                    dve.wait_ge(exp_made, TT * i + t + 1)
                    dve.reciprocal(row_rec[:, t:t + 1], row_sum[:, t:t + 1])
                    dve.drain()
                    dve.tensor_scalar(prob[:, t, 0:n], prob[:, t, 0:n], row_rec[:, t:t + 1], None,
                                      ALU.mult).then_inc(prob_made, 1)

                bias_and_max(0)
                bias_and_max(1)
                divide(0)
                divide(1)
                bias_and_max(2)
                bias_and_max(3)
                divide(2)
                divide(3)

            for n, (y, hi, lo) in enumerate(((y_ssm, ys_hi, ys_lo), (y_attn, ya_hi, ya_lo))):
                for c in range(0, WC, 2):
                    dve.wait_ge(split_hi_made, n * WC // 2 + c // 2 + 1)
                    tt(lo[:, c:c + 2, :], y[:, c:c + 2, :], hi[:, c:c + 2, :].bitcast(F32),
                       ALU.subtract).then_inc(split_lo_made, 1)

            def split(src, hi, lo):
                dve.tensor_copy(hi, src)
                dve.drain()
                return tt(lo, src, hi.bitcast(F32), ALU.subtract)

            with dve.Fori(0, WC // 2) as j:
                for s in range(2):
                    m = 2 * j + s
                    dve.wait_ge(evac, m + 3)
                    at = bass.ds(m, 1)
                    y3 = glu_y[:, :].unsqueeze(1)
                    tt(y3, y_ssm[:, at, :], glu_s[s][:, :].unsqueeze(1), ALU.mult)
                    dve.drain()
                    split(y3, y2_hi[:, at, :], y2_lo[:, at, :]).then_inc(glu_made, 1)
                    dve.drain()

            with dve.Fori(0, DC // 2) as j:
                for s in range(2):
                    d = 2 * j + s
                    dve.wait_ge(sig_made, d + 1)
                    dve.wait_ge(blk_done, BLK_UP + 2 * d + 1)
                    tt(up_a[:, :], ps_p[0][:, :], gates[s][:, 0, :], ALU.mult).then_inc(evac, 1)
                    dve.wait_ge(blk_done, BLK_UP + 2 * d + 2)
                    tt(up_s[:, :], ps_p[1][:, :], gates[s][:, 1, :], ALU.mult).then_inc(evac, 1)
                    dve.drain()
                    tt(up_m[:, :], up_a[:, :], up_s[:, :], ALU.add)
                    dve.drain()
                    at = bass.ds(d, 1)
                    split(up_m[:, :].unsqueeze(1), m_hi[:, at, :], m_lo[:, at, :]).then_inc(merged, 1)
                    dve.drain()

            dve.wait_ge(res_landed, 16 * TT)
            for c in range(4):
                with dve.Fori(2 * c, 2 * c + 2) as j:
                    for s in range(2):
                        o = 2 * j + s
                        dve.wait_ge(mt_turned, o + 3)
                        at = bass.ds(o * P, P)
                        dve.scalar_tensor_tensor(res[:, :, at], res[:, :, at], ALPHA,
                                                 ps_t[s][:, :].rearrange("p (t n) -> p t n", t=TT), ALU.mult,
                                                 ALU.add).then_inc(mt_used, 1)
                dve.drain()
                for t in range(TT):
                    quarter(res, t, c)
            dve.drain()
            dve.wait_ge(ln1_landed, 32)
            normalised(res, ln_g, ln_b, 1)
            turned_lo(h1_lo, h1_hi, 1)
            def top16(src, other, vals, idx, tiles, after=None):
                for t in tiles:
                    dve.max(vals[:, t, 0:8], src(t))
                dve.drain()
                for t in tiles:
                    dve.max_index(idx[:, t, 0:8], vals[:, t, 0:8], src(t))
                for t in tiles:
                    last = dve.match_replace(other(t), vals[:, t, 0:8], src(t), -3.0e38)
                if after is not None:
                    last.then_inc(after, 1)
                dve.drain()
                for t in tiles:
                    dve.max(vals[:, t, 8:16], other(t))
                dve.drain()
                for t in tiles:
                    dve.max_index(idx[:, t, 8:16], vals[:, t, 8:16], other(t))
                dve.drain()

            def best_keys(first, end):
                with dve.Fori(first, end) as j:
                    for s in range(2):
                        o = 2 * j + s
                        dve.wait_ge(mt_turned, N_OUT + o + 3)
                        dve.memset(gate_sum[:, 0:1], 0.0)
                        top16(lambda t: ps_t[s][:, t * P:(t + 1) * P], lambda t: rest[:, t, :], top_v, top_i, range(TT),
                              mt_used)
                        at = bass.ds(o, 1)
                        dve.tensor_copy(v_all[:, :, at, :], top_v[:, :, :].unsqueeze(2))
                        dve.tensor_copy(i_all[:, :, at, :], top_i[:, :, :].unsqueeze(2))
                        dve.drain()

            best_keys(0, RH // 2)
            dve.wait_ge(sq_made, 2 * TT)
            dve.tensor_reduce(sq_tot[:, :], sq_sum[:, :].rearrange("p (t z) -> p t z", z=2), AX.X, ALU.add)
            dve.drain()
            dve.tensor_scalar(sq_tot[:, :], sq_tot[:, :], 1.0 / D, EPS, ALU.mult, ALU.add).then_inc(ms_ready, 1)
            best_keys(RH // 2, RH)
            dve.wait_ge(rms_ready, 1)
            dve.reciprocal(sq_rec[:, :], sq_tot[:, :])
            dve.drain()
            dve.wait_ge(emb_g_landed, 16)
            for t in range(TT):
                dve.scalar_tensor_tensor(emb[:, t, :], emb[:, t, :], sq_rec[:, t:t + 1], emb_g[:, :], ALU.mult,
                                         ALU.mult)
            dve.drain()

            with dve.Fori(0, RH) as j:
                def embed(s):
                    o = 2 * j + s
                    dve.wait_ge(mt_turned, N_OUT + N_Q + o + 3)
                    at = bass.ds(o * P, P)
                    tt(emb_add[:, :, :], ps_t[s][:, :].rearrange("p (t n) -> p t n", t=TT), emb[:, :, at],
                       ALU.mult).then_inc(mt_used, 1)
                    dve.drain()
                    dve.scalar_tensor_tensor(res[:, :, at], res[:, :, at], ALPHA, emb_add[:, :, :], ALU.mult,
                                             ALU.add)
                    dve.drain()

                wide = [P, TT, TOPK, TOPK]
                one, two = bass.ds(2 * j, 1), bass.ds(2 * j + 1, 1)
                tt(cand[:, :, :, :],
                   v_all[:, :, one, :].rearrange("p t a k -> p t (a k)").unsqueeze(3).to_broadcast(wide),
                   v_all[:, :, two, :].to_broadcast(wide), ALU.add)
                dve.drain()

                def best(tiles):
                    top16(lambda t: cand[:, t, :, :].rearrange("p a b -> p (a b)"), lambda t: cand_rest[:, t, :],
                          top_v, top_i, tiles)

                embed(0)
                best(range(0, 2))
                embed(1)
                best(range(2, 4))
                at = bass.ds(j * TOPK, TOPK)
                tt(sel_g[:, :, at], top_v[:, :, :], top_v[:, :, 0:1].to_broadcast([P, TT, TOPK]), ALU.subtract)
                dve.tensor_scalar(pos_a[:, :, :], top_i[:, :, :], 4, None, ALU.logical_shift_right)
                dve.tensor_scalar(pos_b[:, :, :], top_i[:, :, :], 15, None, ALU.bitwise_and)
                dve.drain()
                dve.tensor_copy(pos_af[:, :, :], pos_a[:, :, :])
                dve.tensor_copy(pos_bf[:, :, :], pos_b[:, :, :])
                dve.drain()
                flat = [P, TT * TOPK, TOPK]
                for eq, pos in ((eq_a, pos_af), (eq_b, pos_bf)):
                    tt(eq[:, :, :, :].rearrange("p t k a -> p (t k) a"),
                       iota[:, 0:TOPK].unsqueeze(1).to_broadcast(flat),
                       pos[:, :, :].rearrange("p t k -> p (t k)").unsqueeze(2).to_broadcast(flat), ALU.is_equal)
                dve.drain()
                for eq, half in ((eq_a, one), (eq_b, two)):
                    tt(eq[:, :, :, :], eq[:, :, :, :], i_all[:, :, half, :].to_broadcast(wide), ALU.mult)
                dve.drain()
                for eq, sel in ((eq_a, sel_i), (eq_b, sel_j)):
                    dve.tensor_reduce(sel[:, :, at], eq[:, :, :, :], AX.X, ALU.add)
                dve.drain()
            dve.sem_inc(picks_made, 1)
            dve.wait_ge(exps_made, 1)
            g4 = sel_g[:, :, :].rearrange("p t (r k) -> p (t r) k", k=TOPK)
            dve.tensor_reduce(gate_sum[:, :], g4, AX.X, ALU.add)
            dve.drain()
            dve.reciprocal(gate_rec[:, :], gate_sum[:, :])
            dve.drain()
            tt(g4, g4, gate_rec[:, :].unsqueeze(2).to_broadcast([P, TT * RH, TOPK]), ALU.mult).then_inc(gates_made, 1)
            dve.wait_ge(pick_gh_made, 1)
            tt(pick_gl[:, :], ps_t[0][:, :], pick_gh[:, :].bitcast(F32), ALU.subtract)
            dve.drain()

            with dve.Fori(0, HOT_ITER) as j:
                at = bass.ds(4 * HOT * j, 4 * HOT)
                for z, src in enumerate((pick_i[:, at], pick_j[:, at], pick_gh[:, at].bitcast(F32), pick_gl[:, at])):
                    dve.tensor_copy(cols[:, z, :], src)
                dve.drain()
                for s in range(4):
                    for k in range(HOT):
                        c = HOT * s + k
                        dve.tensor_scalar(hot_j[:, k, :], iota[:, :], cols[:, 1, c:c + 1], None, ALU.is_equal)
                        for z in range(2):
                            last = dve.tensor_scalar(hot_g[:, k, z, :], iota[:, :], cols[:, 0, c:c + 1],
                                                     cols[:, 2 + z, c:c + 1], ALU.is_equal, ALU.mult)
                    last.then_inc(hot_made, 1)
                    dve.wait_ge(hot_moved, 4 * j + s + 1)
                    for m in range(HOT // 2):
                        last = tt(hot_out(s, m), hot_out(s, m), hot_in(m)[:, 1], ALU.add)
                    if s % 2 == 1:
                        last.then_inc(hot_evac, 1)
                    dve.drain()

            def weights_of(sbn, k, landed):
                dve.wait_ge(aux_landed[k], landed)
                tt(ew[:, :, :], act_in[k][:, :, :], gate_in[k][:, :, :].rearrange("p t i -> p i t"), ALU.mult)
                dve.drain()
                if not (isinstance(sbn, int) and sbn == 0):
                    dve.wait_ge(v_done, 16 * (sbn - 1) + 1)
                split(ew[:, :, :], ew_hi[k][:, :, :], ew_lo[k][:, :, :]).then_inc(ew_made, 1)
                dve.drain()

            weights_of(0, 0, 32)

            def expert_pair(j, last):
                for k in range(2):
                    for c in range(4):
                        if c == 3 and not (last and k == 1):
                            weights_of(2 * j + k + 1, (k + 1) % 2, 32 * (j + 1 + k))
                        for t in range(TT):
                            dve.wait_ge(v_done, 4 * (8 * j + 4 * k + c) + t + 2)
                            part = res[:, t, c * 512:(c + 1) * 512]
                            tt(part, part, ps[4 * ((c + 1) % 2) + t][:, :], ALU.add).then_inc(v_added, 1)
                            if last and k == 1 and c == 3:
                                dve.drain()
                                quarter(res, t, c)
                                dve.drain()
                                variance(t)
                                scale(2, t)
                                if t == 0:
                                    dve.wait_ge(ln2_landed, 32)
                                else:
                                    gain(res, ln2_g, 2, t - 1)
                        if last and k == 1 and c < 3:
                            dve.drain()
                            for t in range(TT):
                                quarter(res, t, c)
                    dve.drain()

            with dve.Fori(0, SB // 2 - 1) as j:
                expert_pair(j, False)
            expert_pair(SB // 2 - 1, True)
            gain(res, ln2_g, 2, 3)
            bias(res, ln2_b, 3)


def _blocks(a, chunks):
    return a.reshape(chunks, P, a.shape[1] // P, P).transpose(2, 1, 0, 3)


def _slabs(i):
    order = [b for h in range(HEADS)
             for b in (24 + h, h, 8 + h, 16 + h, 32 + 4 * h, 33 + 4 * h, 34 + 4 * h, 35 + 4 * h)]
    parts = [_blocks(i["w_in"][0], DC)[order].reshape(N_IN, P, SL)]
    glu = _blocks(i["w_ssm_glu"][0], WC).reshape(N_GLU, 2, P, HALF).transpose(0, 2, 1, 3)
    parts.append(glu.reshape(N_GLU, P, SL))
    up = np.stack([_blocks(i["w_attn_up"][0], WC), _blocks(i["w_ssm_up"][0], WC)], 1)
    parts.append(up.transpose(0, 2, 1, 3, 4).reshape(N_UP, P, SL))
    for name in ("w_mix_out", "w_peer_q", "ple_w_gate"):
        parts.append(_blocks(i[name][0], DC).reshape(DC, P, SL))
    parts.append(i["peer_u"][0].reshape(EB, P, DC, P).transpose(0, 3, 2, 1).reshape(N_U, P, SL))
    parts.append(i["peer_v"][0].reshape(SB, 4, P, 4, 512).transpose(0, 3, 2, 1, 4).reshape(N_V, P, SL))
    return np.concatenate(parts, 0)


def _states(a):
    return a.reshape(QN, 2, ST).transpose(1, 2, 0).reshape(P, QN)


def kernel(**inputs):
    import concourse.bacc as bacc
    from concourse.bass_utils import run_bass_kernel_spmd

    i = {k: np.asarray(v) for k, v in inputs.items()}
    rel = i["attn_rel_bias"][0][:, ::-1]
    b_c = np.stack([i["ssm_b_re"][0], i["ssm_b_im"][0]]).reshape(2, QN, 2, ST, GCH)
    c_c = np.stack([i["ssm_c_re"][0], i["ssm_c_im"][0]]).reshape(2, HEADS, CB_Q, 2, GCH, ST)
    names = ("ln_in_g", "ln_in_b", "ln1_g", "ln1_b", "ple_norm_g", "ln2_g", "ln2_b")
    arrays = {
        "x": i["x"][0],
        "p_t": i["p"][0, 0].T.reshape(2, P, S).transpose(1, 0, 2),
        "vecs": np.stack([i[n].reshape(D) for n in names]),
        "weights": _slabs(i),
        "band_ext": np.concatenate([np.repeat(rel[:, :1], P - 1, 1), rel], 1),
        "lam_re": _states(i["ssm_lam_re"][0]),
        "lam_im": _states(i["ssm_lam_im"][0]),
        "log_dt": i["ssm_log_dt"][0].reshape(QN, 2).T,
        "b_in": b_c.transpose(2, 3, 0, 1, 4).reshape(P, 2, QN, GCH),
        "c_in": c_c.transpose(1, 3, 5, 0, 2, 4).reshape(HEADS, P, 2, CB_Q, GCH),
        "d_skip": i["ssm_d"].reshape(W2),
        "keys_t": i["peer_sub_keys"][0].reshape(2 * RH, NK, P).transpose(2, 0, 1),
        "ple_w": i["ple_w_in"][0].reshape(2, P, D).transpose(1, 0, 2),
    }
    arrays = {f"in_{k}": np.ascontiguousarray(v) for k, v in arrays.items()}
    nc = bacc.Bacc("TRN2", target_bir_lowering=False, num_devices=1, dynamic_dma_scratch_size=1024)
    args = {k[3:]: nc.dram_tensor(k, v.shape, F32, kind="ExternalInput").ap() for k, v in arrays.items()}
    out = nc.dram_tensor("out_dram", (S, D), F32, kind="ExternalOutput").ap()
    build_trunk(nc, out=out, **args)
    r = run_bass_kernel_spmd(nc, [arrays], core_ids=[0])
    return r.results[0]["out_dram"].reshape(1, S, D)
```
